# Optimizing a Trainium2 kernel written in Bass

```python
import jax, jax.numpy as jnp
from jax import lax
import numpy as np

D_MODEL = 1024
BATCH = 1
SEQ = 256
DEPTH = 2

GRID_W = 64
CTX_LEN = 256
HEAD_DIM = 64
BRANCH_W = 512
N_BRANCH = 3
A_HEADS = 8
A_KV_HEADS = 2
A_GROUP = A_HEADS // A_KV_HEADS
WINDOW = 128
A_KV_W = A_KV_HEADS * HEAD_DIM
CONV_K = 3
NA_HEADS = 8
NA_ROWS_MAX = 8
NA_COLS = 16
ROPE_BASE = 10000.0
IN_SIZES = (BRANCH_W, A_KV_W, A_KV_W, BRANCH_W, BRANCH_W, BRANCH_W, BRANCH_W, BRANCH_W, BRANCH_W, N_BRANCH * D_MODEL)
IN_COLS = sum(IN_SIZES)
FFN_DENSE = 2816
N_EXPERTS = 8
TOP_K = 2
FFN_EXPERT = 3584
MOE_BLOCK = 128
N_DENSE = (DEPTH + 1) // 2
N_MOE = DEPTH // 2
RMS_EPS = 1e-6

kernel_name = "hybrid_gated_window_conv_natten_moe_dit"

def rmsnorm(x, g):
    xf = x.astype(jnp.float32)
    y = xf * lax.rsqrt(jnp.mean(xf * xf, axis=-1, keepdims=True) + RMS_EPS)
    return (y * g.astype(jnp.float32)).astype(x.dtype)

def modulate(h, shift, scale):
    return h * (1 + scale) + shift

def split_cols(z):
    parts, off = [], 0
    for n in IN_SIZES:
        parts.append(z[..., off:off + n])
        off += n
    return parts

def to_heads(t, n_heads):
    return t.reshape(t.shape[0], t.shape[1], n_heads, HEAD_DIM)

def axial_rope_tables(n_tokens, dtype):
    pos = jnp.arange(n_tokens)
    row = (pos // GRID_W).astype(jnp.float32)
    col = (pos % GRID_W).astype(jnp.float32)
    half = HEAD_DIM // 2
    inv = 1.0 / (ROPE_BASE ** (jnp.arange(0, half, 2, dtype=jnp.float32) / half))
    ar = row[:, None] * inv[None]
    ac = col[:, None] * inv[None]
    ang = jnp.concatenate([ar, ar, ac, ac], axis=-1)[:, None, :]
    return jnp.cos(ang).astype(dtype), jnp.sin(ang).astype(dtype)

def axial_rope(t, cos, sin):
    half, quarter = HEAD_DIM // 2, HEAD_DIM // 4
    def rot(u):
        return jnp.concatenate([-u[..., quarter:], u[..., :quarter]], axis=-1)
    rotated = jnp.concatenate([rot(t[..., :half]), rot(t[..., half:])], axis=-1)
    return t * cos + rotated * sin

def joint_softmax(parts, sink=None):
    m = parts[0].max(axis=-1, keepdims=True)
    for s in parts[1:]:
        m = jnp.maximum(m, s.max(axis=-1, keepdims=True))
    if sink is not None:
        m = jnp.maximum(m, sink)
    es = [jnp.exp(s - m) for s in parts]
    den = es[0].sum(axis=-1, keepdims=True)
    for e in es[1:]:
        den = den + e.sum(axis=-1, keepdims=True)
    if sink is not None:
        den = den + jnp.exp(sink - m)
    return [e / den for e in es]

def window_gqa(q, k, v, kc, vc, sink):
    b, s = q.shape[:2]
    nb = s // WINDOW
    scale = HEAD_DIM ** -0.5
    qb = q.reshape(b, nb, WINDOW, A_KV_HEADS, A_GROUP, HEAD_DIM)
    def band(t):
        tp = jnp.pad(t.reshape(b, nb, WINDOW, A_KV_HEADS, HEAD_DIM), ((0, 0), (1, 1), (0, 0), (0, 0), (0, 0)))
        return jnp.concatenate([tp[:, :-2], tp[:, 1:-1], tp[:, 2:]], axis=2)
    kb, vb = band(k), band(v)
    qpos = jnp.arange(s).reshape(nb, WINDOW)
    kpos = (jnp.arange(nb)[:, None] - 1) * WINDOW + jnp.arange(3 * WINDOW)[None]
    valid = ((jnp.abs(qpos[:, :, None] - kpos[:, None, :]) <= WINDOW)
             & (kpos[:, None, :] >= 0) & (kpos[:, None, :] < s))
    s_win = jnp.einsum('bnqkgd,bnjkd->bnkgqj', qb, kb, preferred_element_type=jnp.float32) * scale
    s_win = jnp.where(valid[None, :, None, None], s_win, -jnp.inf)
    s_ctx = jnp.einsum('bnqkgd,bjkd->bnkgqj', qb, kc, preferred_element_type=jnp.float32) * scale
    sk = sink.astype(jnp.float32).reshape(A_KV_HEADS, A_GROUP)[:, :, None, None]
    p_win, p_ctx = joint_softmax([s_win, s_ctx], sk)
    o = (jnp.einsum('bnkgqj,bnjkd->bnqkgd', p_win.astype(vb.dtype), vb)
         + jnp.einsum('bnkgqj,bjkd->bnqkgd', p_ctx.astype(vc.dtype), vc))
    return o.reshape(b, s, A_HEADS * HEAD_DIM)

def context_gqa(q, k, v, sink):
    b, n = q.shape[:2]
    qg = q.reshape(b, n, A_KV_HEADS, A_GROUP, HEAD_DIM)
    s = jnp.einsum('blkgd,bjkd->bkglj', qg, k, preferred_element_type=jnp.float32) * HEAD_DIM ** -0.5
    sk = sink.astype(jnp.float32).reshape(A_KV_HEADS, A_GROUP)[:, :, None, None]
    (p,) = joint_softmax([s], sk)
    o = jnp.einsum('bkglj,bjkd->blkgd', p.astype(v.dtype), v)
    return o.reshape(b, n, A_HEADS * HEAD_DIM)

def short_conv(x_in, gate_b, gate_c, w):
    u = gate_c * x_in
    v = lax.conv_general_dilated(u, w[:, None, :].astype(u.dtype), window_strides=(1,),
                                 padding=((CONV_K // 2, CONV_K // 2),),
                                 dimension_numbers=('NWC', 'WIO', 'NWC'),
                                 feature_group_count=u.shape[-1])
    return gate_b * v

def neighbourhood_attn(q, k, v, kc, vc, rpb):
    b, s = q.shape[:2]
    rows = s // GRID_W
    kr = min(NA_ROWS_MAX, rows)
    kcn = NA_COLS
    scale = HEAD_DIM ** -0.5
    qg = q.reshape(b, rows, GRID_W, NA_HEADS, HEAD_DIM)
    kg = k.reshape(b, rows, GRID_W, NA_HEADS, HEAD_DIM)
    vg = v.reshape(b, rows, GRID_W, NA_HEADS, HEAD_DIM)
    r = jnp.arange(rows)
    row_idx = jnp.clip(r - kr // 2, 0, rows - kr)[:, None] + jnp.arange(kr)[None]
    k_rows = kg[:, row_idx]
    v_rows = vg[:, row_idx]
    col = jnp.arange(GRID_W)
    col_start = jnp.clip(col - kcn // 2, 0, GRID_W - kcn)
    col_ok = (col[None, :] >= col_start[:, None]) & (col[None, :] < col_start[:, None] + kcn)
    dr = row_idx - r[:, None] + NA_ROWS_MAX - 1
    dc = jnp.clip(col[None, :] - col[:, None], -(kcn - 1), kcn - 1) + kcn - 1
    bias = rpb.astype(jnp.float32)[:, dr[:, None, :, None], dc[None, :, None, :]]
    bias = jnp.where(col_ok[None, None, :, None, :], bias, -jnp.inf).transpose(1, 0, 2, 3, 4)
    s_nb = jnp.einsum('brqhd,brkjhd->brhqkj', qg, k_rows, preferred_element_type=jnp.float32) * scale + bias[None]
    s_nb = s_nb.reshape(b, rows, NA_HEADS, GRID_W, kr * GRID_W)
    s_ctx = jnp.einsum('brqhd,bjhd->brhqj', qg, kc, preferred_element_type=jnp.float32) * scale
    p_nb, p_ctx = joint_softmax([s_nb, s_ctx])
    p_nb = p_nb.reshape(b, rows, NA_HEADS, GRID_W, kr, GRID_W)
    o = (jnp.einsum('brhqkj,brkjhd->brqhd', p_nb.astype(v_rows.dtype), v_rows)
         + jnp.einsum('brhqj,bjhd->brqhd', p_ctx.astype(vc.dtype), vc))
    return o.reshape(b, s, NA_HEADS * HEAD_DIM)

def context_mha(q, k, v):
    s = jnp.einsum('blhd,bjhd->bhlj', q, k, preferred_element_type=jnp.float32) * HEAD_DIM ** -0.5
    (p,) = joint_softmax([s])
    o = jnp.einsum('bhlj,bjhd->blhd', p.astype(v.dtype), v)
    return o.reshape(q.shape[0], q.shape[1], NA_HEADS * HEAD_DIM)

def branch_merge(o_a, o_b, o_c, gate_pre, b_gate, w_branch, w_out):
    o = jnp.stack([o_a, o_b, o_c], axis=-2)
    proj = jnp.einsum('bnrc,rcd->bnrd', o, w_branch)
    g = jax.nn.sigmoid(gate_pre.reshape(*gate_pre.shape[:-1], N_BRANCH, D_MODEL) + b_gate.reshape(N_BRANCH, D_MODEL))
    return jnp.sum(g * proj, axis=-2) @ w_out

def mixer_sublayer(hx, hc, cos, sin, w_in, b_gate, sink, conv_w, rpb, w_branch, w_out, with_ctx_out):
    qa, ka, va, ux, gbx, gcx, qn, kn, vn, gx = split_cols(hx @ w_in)
    qa_c, ka_c, va_c, uc, gbc, gcc, qn_c, kn_c, vn_c, gc = split_cols(hc @ w_in)
    ka_c, va_c = to_heads(ka_c, A_KV_HEADS), to_heads(va_c, A_KV_HEADS)
    kn_c, vn_c = to_heads(kn_c, NA_HEADS), to_heads(vn_c, NA_HEADS)
    o_a = window_gqa(axial_rope(to_heads(qa, A_HEADS), cos, sin), axial_rope(to_heads(ka, A_KV_HEADS), cos, sin),
                     to_heads(va, A_KV_HEADS), ka_c, va_c, sink)
    o_b = short_conv(ux, gbx, gcx, conv_w)
    o_c = neighbourhood_attn(to_heads(qn, NA_HEADS), to_heads(kn, NA_HEADS), to_heads(vn, NA_HEADS), kn_c, vn_c, rpb)
    y_x = branch_merge(o_a, o_b, o_c, gx, b_gate, w_branch, w_out)
    if not with_ctx_out:
        return y_x, None
    o_a_c = context_gqa(to_heads(qa_c, A_HEADS), ka_c, va_c, sink)
    o_b_c = short_conv(uc, gbc, gcc, conv_w)
    o_c_c = context_mha(to_heads(qn_c, NA_HEADS), kn_c, vn_c)
    y_c = branch_merge(o_a_c, o_b_c, o_c_c, gc, b_gate, w_branch, w_out)
    return y_x, y_c

def swiglu(h, w_gu, w_dn):
    g, u = jnp.split(h @ w_gu, 2, axis=-1)
    return (jax.nn.silu(g) * u) @ w_dn

def moe_swiglu(xt, w_router, b_router, w_gu, w_dn):
    t = xt.shape[0]
    logits = (xt @ w_router).astype(jnp.float32) + b_router.astype(jnp.float32)
    top_v, top_e = lax.top_k(logits, TOP_K)
    gates = jax.nn.softmax(top_v, axis=-1)
    n_assign = t * TOP_K
    e_flat = top_e.reshape(-1)
    tok_flat = jnp.repeat(jnp.arange(t, dtype=jnp.int32), TOP_K)
    g_flat = gates.reshape(-1)
    order = jnp.argsort(e_flat)
    e_s, tok_s, g_s = e_flat[order], tok_flat[order], g_flat[order]
    counts = jnp.bincount(e_flat, length=N_EXPERTS)
    padded = (counts + MOE_BLOCK - 1) // MOE_BLOCK * MOE_BLOCK
    start = jnp.cumsum(counts) - counts
    ends = jnp.cumsum(padded)
    pstart = ends - padded
    dest = pstart[e_s] + jnp.arange(n_assign) - start[e_s]
    n_blocks = -(-n_assign // MOE_BLOCK) + N_EXPERTS
    n_rows = n_blocks * MOE_BLOCK
    row_tok = jnp.full((n_rows,), t, jnp.int32).at[dest].set(tok_s)
    row_gate = jnp.zeros((n_rows,), jnp.float32).at[dest].set(g_s)
    block_e = jnp.clip(jnp.searchsorted(ends, jnp.arange(n_blocks) * MOE_BLOCK, side='right'), 0, N_EXPERTS - 1)
    x_pad = jnp.concatenate([xt, jnp.zeros((1, xt.shape[1]), xt.dtype)], axis=0)
    xb = x_pad[row_tok].reshape(n_blocks, MOE_BLOCK, xt.shape[1])
    def expert_block(args):
        xblk, e = args
        g, u = jnp.split(xblk @ w_gu[e], 2, axis=-1)
        return (jax.nn.silu(g) * u) @ w_dn[e]
    yb = lax.map(expert_block, (xb, block_e)).reshape(n_rows, xt.shape[1])
    yb = yb * row_gate[:, None].astype(yb.dtype)
    return jnp.zeros((t + 1, xt.shape[1]), yb.dtype).at[row_tok].add(yb)[:t]

def channel_mixer(h, layer, w_gu_dense, w_dn_dense, w_router, b_router, w_gu_moe, w_dn_moe):
    if layer % 2 == 0:
        return swiglu(h, w_gu_dense[layer // 2], w_dn_dense[layer // 2])
    b, n, d = h.shape
    i = layer // 2
    return moe_swiglu(h.reshape(b * n, d), w_router[i], b_router[i], w_gu_moe[i], w_dn_moe[i]).reshape(b, n, d)

def setup_inputs(seed: int = 0) -> dict:
    key = jax.random.key(seed)
    ks = jax.random.split(key, 24)
    D = D_MODEL
    def nrm(k, shape, s):
        return jax.random.normal(k, shape, jnp.float32) * s
    return {
        "x": nrm(ks[0], (BATCH, SEQ, D), 1.0),
        "c": nrm(ks[1], (BATCH, D), 1.0),
        "ctx": nrm(ks[2], (BATCH, CTX_LEN, D), 1.0),
        "c_ctx": nrm(ks[3], (D,), 1.0),
        "w_ada": nrm(ks[4], (DEPTH, D, 6 * D), 0.5 * D ** -0.5),
        "b_ada": nrm(ks[5], (DEPTH, 6 * D), 0.02),
        "g_pre_mix": 1.0 + nrm(ks[6], (DEPTH, D), 0.02),
        "g_post_mix": 1.0 + nrm(ks[7], (DEPTH, D), 0.02),
        "g_pre_ffn": 1.0 + nrm(ks[8], (DEPTH, D), 0.02),
        "g_post_ffn": 1.0 + nrm(ks[9], (DEPTH, D), 0.02),
        "w_in": nrm(ks[10], (DEPTH, D, IN_COLS), D ** -0.5),
        "b_gate": nrm(ks[11], (DEPTH, N_BRANCH * D), 0.02),
        "sink": nrm(ks[12], (DEPTH, A_HEADS), 0.5),
        "conv_w": nrm(ks[13], (DEPTH, CONV_K, BRANCH_W), CONV_K ** -0.5),
        "rpb": nrm(ks[14], (DEPTH, NA_HEADS, 2 * NA_ROWS_MAX - 1, 2 * NA_COLS - 1), 0.1),
        "w_branch": nrm(ks[15], (DEPTH, N_BRANCH, BRANCH_W, D), BRANCH_W ** -0.5),
        "w_out": nrm(ks[16], (DEPTH, D, D), D ** -0.5),
        "w_gu_dense": nrm(ks[17], (N_DENSE, D, 2 * FFN_DENSE), D ** -0.5),
        "w_dn_dense": nrm(ks[18], (N_DENSE, FFN_DENSE, D), FFN_DENSE ** -0.5),
        "w_router": nrm(ks[19], (N_MOE, D, N_EXPERTS), D ** -0.5),
        "b_router": nrm(ks[20], (N_MOE, N_EXPERTS), 0.01),
        "w_gu_moe": nrm(ks[21], (N_MOE, N_EXPERTS, D, 2 * FFN_EXPERT), D ** -0.5),
        "w_dn_moe": nrm(ks[22], (N_MOE, N_EXPERTS, FFN_EXPERT, D), FFN_EXPERT ** -0.5),
    }

def reference(x, c, ctx, c_ctx, w_ada, b_ada, g_pre_mix, g_post_mix, g_pre_ffn, g_post_ffn, w_in, b_gate,
              sink, conv_w, rpb, w_branch, w_out, w_gu_dense, w_dn_dense, w_router, b_router, w_gu_moe, w_dn_moe):
    cos, sin = axial_rope_tables(x.shape[1], x.dtype)
    h_ctx = ctx
    for l in range(DEPTH):
        update_ctx = l < DEPTH - 1
        mod_x = (jax.nn.silu(c) @ w_ada[l] + b_ada[l])[:, None, :]
        mod_c = jax.nn.silu(c_ctx) @ w_ada[l] + b_ada[l]
        sh1, sc1, gt1, sh2, sc2, gt2 = jnp.split(mod_x, 6, axis=-1)
        csh1, csc1, cgt1, csh2, csc2, cgt2 = jnp.split(mod_c, 6, axis=-1)
        hx = modulate(rmsnorm(x, g_pre_mix[l]), sh1, sc1)
        hc = modulate(rmsnorm(h_ctx, g_pre_mix[l]), csh1, csc1)
        y_x, y_c = mixer_sublayer(hx, hc, cos, sin, w_in[l], b_gate[l], sink[l], conv_w[l], rpb[l],
                                  w_branch[l], w_out[l], update_ctx)
        x = x + gt1 * rmsnorm(y_x, g_post_mix[l])
        hx = modulate(rmsnorm(x, g_pre_ffn[l]), sh2, sc2)
        x = x + gt2 * rmsnorm(channel_mixer(hx, l, w_gu_dense, w_dn_dense, w_router, b_router, w_gu_moe, w_dn_moe), g_post_ffn[l])
        if update_ctx:
            h_ctx = h_ctx + cgt1 * rmsnorm(y_c, g_post_mix[l])
            hc = modulate(rmsnorm(h_ctx, g_pre_ffn[l]), csh2, csc2)
            h_ctx = h_ctx + cgt2 * rmsnorm(channel_mixer(hc, l, w_gu_dense, w_dn_dense, w_router, b_router, w_gu_moe, w_dn_moe), g_post_ffn[l])
    return x


_drawn_inputs = setup_inputs


def setup_inputs(seed=0):
    import zlib

    import numpy as np

    out = dict(_drawn_inputs(seed))
    spreads = {}
    factors = {'g_post_mix': 2.933,
     'g_post_ffn': 6.484,
     'b_gate': 3.424,
     'sink': 8.0,
     'rpb': 8.0,
     'b_router': 3.46}
    for name, (base, spread) in spreads.items():
        noise = np.random.default_rng([zlib.crc32(name.encode()), seed]).standard_normal(out[name].shape)
        drawn = base * np.exp(spread * noise) if base else spread * noise
        out[name] = __import__('jax').numpy.asarray(drawn.astype(out[name].dtype))
    for name, factor in factors.items():
        out[name] = (out[name] * factor).astype(out[name].dtype)
    return out
```

```python
import numpy as np
import concourse.bass as bass
from concourse import mybir
from contextlib import ExitStack

F32 = mybir.dt.float32
F32R = mybir.dt.float32r
I32 = mybir.dt.int32
ALU = mybir.AluOpType
ACT = mybir.ActivationFunctionType
AX = mybir.AxisListType

P = 128
D = 1024
KT = D // P
SEQ = 256
TOK = 512
HD = 64
BW = 512
BT = BW // P
DEPTH = 2
WINDOW = 128
GRID_W = 64
NA_COLS = 16
RPB_R, RPB_C = 15, 31
FFN_D = 2816
FFN_E = 3584
NE = 8
EPS = 1e-6
BIG = 1e30

F_HALF = (12, 10)
GU_SLABS = 2 * FFN_E // 256
GU_GROUPS = GU_SLABS // 2
FE_T = FFN_E // P
DN_SLABS = FE_T // 2
JOB_SLABS = GU_SLABS + DN_SLABS
RAW_E, SPLIT_E = 6, 3
MAX_JOBS = 2 * SEQ // P + NE - 1

V_GPRE, V_GPOST, V_GPREF, V_GPOSTF, V_BGATE, V_BADA, V_CONV, V_SINK = 0, 8, 16, 24, 32, 56, 104, 116
V_ALL = 124


def mixer_plan():
    slabs, steps = [], []

    def slab(array, *tiles):
        slabs.append(array)
        for n, (what, i) in enumerate(tiles):
            steps.append((what, i, 2 * (len(slabs) - 1) + n))

    slab("main", ("ka", 0), ("va", 0))
    steps += [("rope_k", 0, None), ("va_t", 0, None)]
    for i in (0, 2):
        slab("main", ("qa", i), ("qa", i + 1))
        steps += [("rope_q", i, None), ("rope_q", i + 1, None)]
    head = len(steps)
    for c in range(BT):
        slab("main", ("ux", c), ("gc", c))
    for c in (0, 2):
        slab("main", ("gb", c), ("gb", c + 1))
    for i in (0, 2):
        slab("main", ("qn", i), ("qn", i + 1))
    for i in (0, 2):
        slab("main", ("kn", i), ("kn", i + 1))
    for s in range(2):
        slabs.append("main")
        u = 2 * (len(slabs) - 1)
        steps += [("vn", (s, 0), u), ("vn", (s, 1), u)]
    mid = len(steps)
    for r in range(3):
        for n in range(0, KT, 2):
            slab("main", ("gx", (r, n)), ("gx", (r, n + 1)))
            slab("br", ("br", (r, n)), ("br", (r, n + 1)))
        if r == 1:
            end = len(steps)
    for n in range(0, KT, 2):
        slab("main", ("wout", n), ("wout", n + 1))
    return slabs, steps, head, mid, end


M_SLABS, M_STEPS, M_HEAD, M_MID, M_END = mixer_plan()
ADA_SLABS = 24
DN_STAGE = KT


def spread(steps, slots):
    out, done = [], 0
    for n, st in enumerate(steps):
        want = (n + 1) * slots // len(steps)
        out.append((list(range(done, want)), st))
        done = want
    return out


def build_program(nc, a, out):
    ctx = ExitStack()
    with ctx:
        def sb(name, shape, dt=F32):
            return ctx.enter_context(nc.sbuf_tensor(name, shape, dt))

        def sem(name):
            return ctx.enter_context(nc.semaphore(name))

        raw = sb("raw", [P, 2, 2048])
        wsp = sb("wsp", [P, 4, 2, 1024], F32R)
        hx = sb("hx", [P, 2, KT, TOK], F32R)
        opr = sb("opr", [P, 12288], F32R)
        xm = sb("xm", [P, KT, TOK])
        M = sb("M", [P, 14336])

        def view(t, at, *shape):
            n = int(np.prod(shape))
            v = t[:, at:at + n]
            if len(shape) == 2:
                v = v.rearrange("p (a b) -> p a b", b=shape[1])
            if len(shape) == 3:
                v = v.rearrange("p (a b c) -> p a b c", b=shape[1], c=shape[2])
            return v

        o_br = [view(opr, 4096 * r, 2, BT, TOK) for r in range(3)]
        m_sp = view(opr, 0, 2, KT, TOK)
        hF = view(opr, 0, 2, 12, TOK)
        qa = view(M, 0, BT, TOK)
        ka = view(M, 2048, TOK)
        V = view(M, 2560, 4, P + BW)
        qn = view(M, 5120, BT, TOK)
        kn = view(M, 7168, BT, TOK)
        cv = view(M, 5120, BT, TOK)
        cu = view(M, 7168, 2, TOK)
        ob = view(M, 8192, 2, TOK)
        vat = view(M, 8192, TOK)
        cw = view(M, 9216, TOK)
        y = view(M, 5120, KT, TOK)
        bias = view(M, 9216, 2, 2, 256)
        hf2 = view(M, 9216, 2, TOK)
        pr = view(M, 10240, 2, TOK)
        sq = view(M, 10240, 2, TOK)
        adr = M[0:4, 10240:10240 + 512].rearrange("p (a b) -> p a b", a=2)
        prT = view(M, 11264, 2, 4, P)
        rs = view(M, 11264, TOK)
        sd = view(M, 11776, TOK)
        q2 = view(M, 12288, 2, 2, P)
        gt = view(M, 12800, 2, TOK)
        tmp = view(M, 13824, TOK)
        hfa = view(M, 0, KT, SEQ)
        yacc = view(M, 0, KT, SEQ)
        ht = view(M, 2048, 2, D)
        yb = view(M, 4096, D)
        tge = view(M, 5120, 2, 256)
        hse = view(M, 5632, 2, 256)
        oh = view(M, 6144, 2, P)
        ohg = view(M, 6400, 2, P)
        ohT = view(M, 6656, SEQ)
        oh2 = view(M, 6912, 2, P)
        raw_e = [raw[:, 0, :].rearrange("p (a b) -> p a b", a=8), raw[:, 1, :].rearrange("p (a b) -> p a b", a=8),
                 view(M, 8192, 8, 256), view(M, 10240, 8, 256), view(M, 12288, 8, 256), xm[:, :, SEQ:TOK]]
        wse = [view(opr, 4096 * n, 2, 8, 256) for n in range(SPLIT_E)]
        xg = [hx[:, h, 0:2, :].rearrange("p a (b c) -> p (a b) c", c=P) for h in range(2)]
        wflat = wsp[:].rearrange("p a b c -> p (a b c)")
        hT = [wflat[:, h * FE_T * P:(h + 1) * FE_T * P].rearrange("p (a b) -> p a b", b=P) for h in range(2)]

        ident = sb("ident", [P, P])
        rot = sb("rot", [P, P])
        ctab = sb("ctab", [P, 2, SEQ])
        tri, ones, iota = ctab[:, 0, 0:P], ctab[:, 0, P:2 * P], ctab[:, 1, 0:P]
        iota8, iota8b, iotaj = ctab[:, 1, P:P + 8], ctab[:, 1, P + 8:P + 16], ctab[0:1, 1, P + 16:P + 16 + 12]
        wmask = sb("wmask", [P, 2, P])
        cmask = sb("cmask", [P, GRID_W])
        mean = sb("mean", [P, P])
        sel = sb("sel", [4, 2])
        eps = sb("eps", [P, 1])
        vec = sb("vec", [P, 2, V_ALL])
        cc = sb("cc", [P, KT, 2])
        cf = sb("cf", [P, KT, 2])
        c4 = sb("c4", [P, KT, 4], F32R)
        mod = sb("mod", [P, 6, KT, 2])
        am = sb("am", [P, 4, KT, 2])
        bgh = sb("bgh", [P, 24])
        st = sb("st", [P, 4, 5])
        wr = sb("wr", [P, KT, NE])
        br = sb("br", [P, NE])
        rt = view(M, 7168, 1024)
        jobs = sb("jobs", [1, 16], I32)

        pp = [ctx.enter_context(nc.psum_tensor(f"pp{i}", [P, 512], F32)) for i in range(2)]
        S = [ctx.enter_context(nc.psum_tensor(f"S{i}", [P, 512], F32)) for i in range(2)]
        T = [ctx.enter_context(nc.psum_tensor(f"T{i}", [P, 512], F32)) for i in range(2)]
        O = [ctx.enter_context(nc.psum_tensor(f"O{i}", [P, 512], F32)) for i in range(2)]

        raw_full = [sem(f"raw_full{i}") for i in range(2)]
        hi_done, lo_done = sem("hi_done"), sem("lo_done")
        tile_done = sem("tile_done")
        taken = [sem(f"taken{i}") for i in range(2)]
        consts_in, vec_in = sem("consts_in"), sem("vec_in")
        x_in, x_back, rc_in = sem("x_in"), sem("x_back"), sem("rc_in")
        c_ready, eps_ready = sem("c_ready"), sem("eps_ready")
        row_copied, cols_done, mod_ready = sem("row_copied"), sem("cols_done"), sem("mod_ready")
        sq_done, sum_done, sd_done = sem("sq_done"), sem("sum_done"), sem("sd_done")
        scaled, affine, h_split = sem("scaled"), sem("affine"), sem("h_split")
        x_upd = sem("x_upd")
        conv_done, ob_split, m_split = sem("conv_done"), sem("ob_split"), sem("m_split")
        q2_ready, scores_done, pre_done, exp_done = sem("q2_ready"), sem("scores_done"), sem("pre_done"), sem("exp_done")
        probs_done, pT_done, pT_copied, pv_done = sem("probs_done"), sem("pT_done"), sem("pT_copied"), sem("pv_done")
        o_hi, o_split = sem("o_hi"), sem("o_split")
        bias_in, bias_ready = [sem("bias_in0"), sem("bias_in1")], sem("bias_ready")
        tanh_done, gu_taken, hF_done = sem("tanh_done"), sem("gu_taken"), sem("hF_done")
        act_self, dve_self, pool_self = sem("act_self"), sem("dve_self"), sem("pool_self")
        rt_pe, rt_act, rt_dve, routed, ht_copied = sem("rt_pe"), sem("rt_act"), sem("rt_dve"), sem("routed"), sem("ht_copied")
        yacc_zero = sem("yacc_zero")
        e_raw = [sem(f"e_raw{i}") for i in range(RAW_E)]
        e_hi, e_lo, e_used = sem("e_hi"), sem("e_lo"), sem("e_used")
        e_onehot, e_gath, e_ohT, e_xghi, e_xg = sem("e_onehot"), sem("e_gath"), sem("e_ohT"), sem("e_xghi"), sem("e_xg")
        e_tanh, e_h, e_T, e_hThi, e_hT = sem("e_tanh"), sem("e_h"), sem("e_T"), sem("e_hThi"), sem("e_hT")
        e_yb, e_scat, e_acc = sem("e_yb"), sem("e_scat"), sem("e_acc")
        out_done = sem("out_done")

        g_ada, g_mix, g_ffn = [0, 0], [0, 0], 0
        g = 0
        order = []
        nmain = nbr = 0

        def add(array, n, width):
            nonlocal nmain, nbr
            for _ in range(n):
                if array == "main":
                    order.append(("main", nmain, width))
                    nmain += 1
                elif array == "br":
                    order.append(("br", nbr, width))
                    nbr += 1
                else:
                    order.append(array + (width,))

        g_ada[0] = len(order)
        add("main", ADA_SLABS, 2048)
        g_mix[0] = len(order)
        for s in M_SLABS:
            add(s, 1, 2048 if s == "main" else 1024)
        g_gu, g_dn = [0, 0], [0, 0]
        for h in range(2):
            g_gu[h] = len(order)
            add("main", F_HALF[h], 2048)
            g_dn[h] = len(order)
            for n in range(DN_STAGE):
                add((f"dn{h}", n), 1, F_HALF[h] * P)
        g_ada[1] = len(order)
        add("main", ADA_SLABS, 2048)
        g_mix[1] = len(order)
        for s in M_SLABS:
            add(s, 1, 2048 if s == "main" else 1024)
        N_SLABS = len(order)
        N_UNITS = 2 * N_SLABS
        width = [w // 2 for _, _, w in order for _ in range(2)]
        last_use = [0] * N_UNITS
        t = 0
        use = [0, 0]
        t_ada, t_gu, t_dn, use_ada, use_dn = [0, 0], [0, 0], [0, 0], [0, 0], [0, 0]
        mixer_steps = [[], []]
        slot_base = {}

        def plan_ada(l):
            nonlocal t
            t_ada[l], use_ada[l] = t, use[0]
            for n in range(2 * ADA_SLABS):
                last_use[2 * g_ada[l] + n] = t = t + 1
            for b in range(2):
                use[b] += ADA_SLABS // 2

        def plan_mixer(l):
            nonlocal t
            nq = TOK if l == 0 else SEQ
            units = (nq // P) * 8
            rows = []
            flow = [([], s) for s in M_STEPS[:M_HEAD]]
            flow += [([(0, k) for k in sl], s) for sl, s in spread(M_STEPS[M_HEAD:M_MID], units + 5)]
            flow += [([(1, k) for k in sl], s) for sl, s in spread(M_STEPS[M_MID:M_END], units + 5)]
            flow += [([], s) for s in M_STEPS[M_END:]]
            bank = 0
            for slots, (what, i, u) in flow:
                if what == "vn" and l == 9:
                    continue
                gu = None if u is None else 2 * g_mix[l] + u
                t += 1
                use[bank] += 1
                if gu is not None:
                    last_use[gu] = t
                    if what == "vn":
                        last_use[gu + 1] = t
                rows.append(dict(slots=slots, what=what, i=i, u=gu, t=t, bank=bank, use=use[bank], l=l))
                bank = 1 - bank
            assert len(rows) % 2 == 0
            mixer_steps[l] = rows

        plan_ada(0)
        plan_mixer(0)
        for h in range(2):
            t_gu[h] = t
            for n in range(2 * F_HALF[h]):
                last_use[2 * g_gu[h] + n] = t = t + 1
            t_dn[h], use_dn[h] = t, use[0]
            for n in range(2 * DN_STAGE):
                last_use[2 * g_dn[h] + n] = t = t + 1
            for b in range(2):
                use[b] += DN_STAGE // 2
        plan_ada(1)
        plan_mixer(1)
        T_DENSE, USE_DENSE = t, list(use)
        step_of = {(l, r["what"], r["i"]): r for l in range(2) for r in mixer_steps[l]}

        def attn_units(l):
            return [(tt, half, qt) for tt in range(4) for half in range(2) for qt in range((TOK if l == 0 else SEQ) // P)]

        unit_base, otile_base, head_base = {}, {}, {}
        ub = ob_ = 0
        for l in range(2):
            for b in range(2):
                unit_base[l, b], otile_base[l, b], head_base[l, b] = ub, ob_, 8 * l
                ub += len(attn_units(l))
                ob_ += 4

        def wait_taken(eng, row):
            eng.wait_ge(taken[row["bank"]], row["use"])

        class Own:
            def __init__(self, eng, s):
                self.eng, self.s, self.base, self.k = eng, s, 0, 0

            def mark(self, ins):
                ins.then_inc(self.s, 1)
                self.k += 1
                return self.base + self.k

            def link(self, ins):
                self.eng.wait_ge(self.s, self.mark(ins))

        def loop(eng, n, body, own=None, first=False):
            k0 = 0
            if first:
                body(0, False)
                k0 = 1
            if own:
                own.base, own.k = own.base + own.k, 0
                start = own.base
            per = [0]
            with eng.Fori(k0, n - 1) as i:
                if own:
                    own.base = start + (i - k0) * body.own_per
                body(i, False)
                if own:
                    per[0] = own.k
                    assert own.k == body.own_per, own.k
            if own:
                own.base, own.k = start + (n - 1 - k0) * per[0], 0
            body(n - 1, True)

        block = ctx.enter_context(nc.Block())

        @block.sync
        def _(sp):
            src = {"main": a["w_main"], "br": a["w_br"], "dn0": a["w_dn0"], "dn1": a["w_dn1"]}
            sp.dma_start(vec[:], a["vec"]).then_inc(vec_in, 16)
            sp.dma_start(cc[:], a["c_both"]).then_inc(vec_in, 16)

            def load(g, slot, arr, idx, w):
                sp.wait_ge(lo_done, 2 * g - 2)
                sp.dma_start(raw[:, slot, 0:w], src[arr][bass.ds(idx, 1), :, :].rearrange("a p n -> (a p) n")
                             ).then_inc(raw_full[slot], 16)

            for g in range(2):
                arr, idx, w = order[g]
                sp.dma_start(raw[:, g, 0:w], src[arr][idx, :, :]).then_inc(raw_full[g], 16)
            sp.dma_start(xm[:], a["x_both"]).then_inc(x_in, 16)
            sp.dma_start(ident[:], a["ident"]).then_inc(consts_in, 16)
            sp.dma_start(rot[:], a["rot"]).then_inc(consts_in, 16)
            sp.dma_start(ctab[:], a["cossin"]).then_inc(consts_in, 16)
            sp.dma_start(wmask[:], a["wmask"]).then_inc(consts_in, 16)
            sp.dma_start(cmask[:], a["cmask"]).then_inc(consts_in, 16)
            sp.dma_start(wr[:], a["w_router"]).then_inc(consts_in, 16)
            sp.dma_start(br[:], a["b_router"]).then_inc(consts_in, 16)
            g = 2
            while g < N_SLABS:
                n = 1
                pair = order[g:g + 2]
                if len(pair) == 2:
                    step = [(order[g + 2 + k][1] - order[g + k][1]) if g + 2 + k < N_SLABS else 0 for k in range(2)]
                    while g + 2 * n + 1 < N_SLABS and all(
                            order[g + 2 * n + k] == (pair[k][0], pair[k][1] + n * step[k], pair[k][2]) for k in range(2)):
                        n += 1
                if len(pair) == 2 and n > 1:
                    with sp.Fori(0, n) as i:
                        for k in range(2):
                            load(g + k + 2 * i, (g + k) % 2, pair[k][0], pair[k][1] + step[k] * i, pair[k][2])
                    g += 2 * n
                else:
                    load(g, g % 2, *order[g])
                    g += 1
            sp.wait_ge(routed, 1)
            n_jobs = sp.value_load(jobs[0:1, 12:13], min_val=1, max_val=MAX_JOBS)
            with sp.Fori(0, n_jobs) as j:
                e = sp.value_load(jobs[0:1, bass.ds(j, 1)], min_val=0, max_val=NE - 1)
                for i in range(JOB_SLABS):
                    sp.wait_ge(e_lo, j * JOB_SLABS + (i + 1))
                    sp.dma_start(raw_e[i % RAW_E], a["w_moe"][bass.ds(e * JOB_SLABS + i, 1), :, :, :]
                                 .rearrange("a p b n -> (a p) b n")).then_inc(e_raw[i % RAW_E], 16)
            sp.wait_ge(x_upd, 8 * 4)
            sp.dma_start(out, xm[:, :, 0:SEQ]).then_inc(out_done, 16)
            sp.wait_ge(out_done, 16)

        @block.gpsimd
        def _(pool):
            own = Own(pool, pool_self)
            pool.memset(eps[:], EPS).then_inc(eps_ready, 1)
            pool.memset(mean[:], 1.0 / D).then_inc(eps_ready, 1)
            own.link(pool.memset(sel[:], 0.0))
            own.link(pool.affine_select(out=sel[:], in_=sel[:], compare_op=ALU.not_equal, fill=1.0,
                                        base=0, pattern=[[-1, 2]], channel_multiplier=1))
            pool.affine_select(out=sel[:], in_=sel[:], compare_op=ALU.not_equal, fill=1.0,
                               base=-2, pattern=[[-1, 2]], channel_multiplier=1).then_inc(eps_ready, 1)

            own.link(pool.memset(q2, 0.0))

            def load_bias(l, head):
                pool.dma_start(bias[:, head % 2, :, :], a["rpb_rows"][l, head]).then_inc(bias_in[head % 2], 16)

            for l in range(2):
                nq = TOK if l == 0 else SEQ
                streams = [(0, SEQ), (SEQ, TOK)][:nq // SEQ]
                for row in mixer_steps[l]:
                    for b, s in row["slots"]:
                        units = attn_units(l)
                        if s >= len(units):
                            continue
                        tt, half, qt = units[s]
                        w = unit_base[l, b] + s
                        if b == 1 and qt == 0:
                            head = 2 * tt + half
                            if head == 0:
                                pool.wait_ge(h_split, 8 * (2 * l + 1))
                                load_bias(l, 0)
                            if head + 1 < 8:
                                if head >= 1:
                                    pool.wait_ge(pre_done, w - (nq // P) + 2)
                                load_bias(l, head + 1)
                            pool.wait_ge(bias_in[head % 2], 16 * (4 * l + head // 2 + 1))
                            bv = bias[:, head % 2, :, :].rearrange("p a (b c) -> p (a b) c", c=GRID_W)
                            cm = cmask[:].rearrange("p (a c) -> p a c", a=1).to_broadcast([P, 8, GRID_W])
                            pool.tensor_tensor(bv, bv, cm, ALU.add).then_inc(bias_ready, 1)
                            pool.wait_ge(bias_ready, head_base[l, b] + head + 1)
                        wait_taken(pool, step_of[l, "rope_q" if b == 0 else "qn", tt])
                        if w >= 2:
                            pool.wait_ge(scores_done, w - 1)
                        src = (qa if b == 0 else qn)[64 * half:64 * half + 64, tt, P * qt:P * qt + P]
                        pool.tensor_copy(q2[64 * half:64 * half + 64, half, w % 2, :], src).then_inc(q2_ready, 1)
                        pool.wait_ge(q2_ready, w + 1)
                    if row["what"] == "gc":
                        c = row["i"]
                        wait_taken(pool, row)
                        wv = lambda k: vec[:, l, V_CONV + 4 * k + c:V_CONV + 4 * k + c + 1]
                        u = cu[:, c % 2, :]
                        own.link(pool.tensor_scalar(cv[:, c, 0:nq], u[:, 0:nq], wv(1), None, ALU.mult))
                        for k, to, fr in ((0, 1, 0), (2, 0, 1)):
                            own.link(pool.tensor_scalar(cw[:, 0:nq], u[:, 0:nq], wv(k), None, ALU.mult))
                            for s0, s1 in streams:
                                v = cv[:, c, s0 + to:s1 - fr]
                                ins = pool.tensor_tensor(v, v, cw[:, s0 + fr:s1 - to], ALU.add)
                                if k == 2 and s1 == nq:
                                    ins.then_inc(conv_done, 1)
                                    pool.wait_ge(conv_done, 4 * l + c + 1)
                                else:
                                    own.link(ins)
            pool.wait_ge(routed, 1)
            pool.memset(yacc, 0.0).then_inc(yacc_zero, 1)
            pool.wait_ge(yacc_zero, 1)

        @block.scalar
        def _(act):
            own = Own(act, act_self)
            nxt = [0]

            def split_hi(u, slot, half, w, gval, tdep):
                if half == 0:
                    act.wait_ge(raw_full[slot // 2], gval)
                if tdep is not None:
                    act.wait_ge(tile_done, tdep)
                act.activation(wsp[:, slot, 0, 0:w], raw[:, slot // 2, half * w:half * w + w], ACT.Copy
                               ).then_inc(hi_done, 1)

            def split_to(u):
                while nxt[0] <= u and nxt[0] < N_UNITS:
                    n = nxt[0]
                    split_hi(n, n % 4, n % 2, width[n], 16 * (n // 4 + 1), last_use[n - 4] if n >= 4 else None)
                    nxt[0] += 1

            def stage_ahead(u0, g0, t0, w, i, s, last):
                if last and s == 1:
                    split_to(nxt[0] + 1)
                    return
                for h in range(2):
                    ur = 2 * (s + 1) + h
                    slot = (u0 + ur) % 4
                    td = t0 + 4 * i + ur - 3
                    if isinstance(td, int) and td < 1:
                        td = None
                    split_hi(None, slot, h, w, 16 * ((u0 + ur) // 4 + 1) + 16 * i, td)
                if last:
                    nxt[0] += 2

            act.wait_ge(vec_in, 32)
            act.activation(cf[:], cc[:], ACT.Tanh, scale=0.5).then_inc(c_ready, 1)

            def ada(l):
                u0, t0 = 2 * g_ada[l], t_ada[l]
                split_to(u0 + 1)

                def body(i, last):
                    for s in range(2):
                        stage_ahead(u0, None, t0, 1024, i, s, last)
                    for s in range(2):
                        act.wait_ge(tile_done, t0 + 4 * i + 2 * s + 2)
                        act.activation(adr[:, s, :], pp[s][0:4, 0:256], ACT.Copy).then_inc(taken[s], 1)
                body.own_per = 0
                n = ADA_SLABS // 2
                keep = nxt[0]
                nxt[0] = u0 + 4 * (n - 1) + 2
                loop(act, n, body, None, first=(l == 0))

            def norm_root(n, N):
                act.wait_ge(sum_done, 8 * (n + 1))
                act.activation(sd[:, 0:N], O[1][:, 0:N], ACT.Sqrt, bias=eps[:]).then_inc(sd_done, 1)

            def square(src, n, k, N):
                if 8 * n + k >= 2:
                    act.wait_ge(sum_done, 8 * n + k - 1)
                act.activation(sq[:, k % 2, 0:N], src, ACT.Square).then_inc(sq_done, 1)

            def prenorm(n, l, which, N, hcount):
                if n in (0, 4):
                    act.wait_ge(cols_done, ADA_SLABS * (l + 1))
                for k in range(KT):
                    if n == 0:
                        if k == 0:
                            act.wait_ge(x_in, 16)
                            act.wait_ge(eps_ready, 3)
                    else:
                        act.wait_ge(x_upd, 8 * hcount[0] + k + 1)
                    square(xm[:, k, 0:N], n, k, N)
                norm_root(n, N)
                act.wait_ge(mod_ready, l + 1)
                for k in range(KT):
                    act.wait_ge(scaled, 8 * pn[0] + k + 1)
                    if 8 * hcount[1] + k >= 2 :
                        act.wait_ge(h_split, max(8 * hcount[1] + k - 1, 0))
                    for s in range(N // SEQ):
                        dst = hfa[:, k, :] if which == 1 and l == 1 else hf2[:, k % 2, SEQ * s:SEQ * s + SEQ]
                        act.activation(dst, gt[:, k % 2, SEQ * s:SEQ * s + SEQ], ACT.Identity,
                                       scale=am[:, 2 * which, k, s:s + 1],
                                       bias=mod[:, 3 * which, k, s:s + 1]).then_inc(affine, 1)
                pn[0] += 1

            pn = [0]

            def attn(l, b, s):
                units = attn_units(l)
                nqt = (TOK if l == 0 else SEQ) // P
                if s < len(units):
                    tt, half, qt = units[s]
                    w = unit_base[l, b] + s
                    n = TOK if qt < 2 else SEQ
                    sc = st[:, w % 4, :]
                    act.wait_ge(pre_done, w + 1)
                    if b == 0:
                        head = tt + 4 * half
                        own.link(act.activation(sc[:, 3:4], vec[:, l, V_SINK + head:V_SINK + head + 1], ACT.Exp, bias=sc[:, 1:2]))
                    if w >= 2:
                        act.wait_ge(pT_done, w - 1)
                    act.activation(pr[:, w % 2, 0:n], S[w % 2][:, 0:n], ACT.Exp, bias=sc[:, 1:2],
                                   accum_out=sc[:, 2:3]).then_inc(exp_done, 1)
                if 0 <= s - 2 < len(units):
                    w = unit_base[l, b] + s - 2
                    kts = 4 if units[s - 2][2] < 2 else 2
                    act.wait_ge(pT_done, w + 1)
                    if w >= 2:
                        act.wait_ge(pv_done, w - 1)
                    act.activation(prT[:, w % 2, 0:kts, :], T[w % 2][:, 0:kts * P].rearrange("p (a b) -> p a b", b=P),
                                   ACT.Copy).then_inc(pT_copied, 1)
                if 0 <= s - 4 < len(units) and (s - 4) % (2 * nqt) == 2 * nqt - 1:
                    tt = units[s - 4][0]
                    ot = otile_base[l, b] + tt
                    act.wait_ge(pv_done, unit_base[l, b] + s - 3)
                    act.activation(o_br[2 * b][:, 0, tt, 0:nqt * P], O[ot % 2][:, 0:nqt * P], ACT.Copy).then_inc(o_hi, 1)

            def mixer(l, nn, hcount):
                nq = TOK if l == 0 else SEQ
                for row in mixer_steps[l]:
                    for b, s in row["slots"]:
                        attn(l, b, s)
                    what, i, u, bank = row["what"], row["i"], row["u"], row["bank"]
                    if u is not None:
                        split_to(u + 2 + (what == "vn"))
                    src = pp[bank]

                    def take(dst, s=None, scale=1.0, func=ACT.Copy, **kw):
                        act.wait_ge(tile_done, row["t"])
                        act.activation(dst, s if s is not None else src[:, 0:nq], func, scale=scale, **kw
                                       ).then_inc(taken[bank], 1)
                    if what == "ka":
                        take(ka, src[:, :])
                    elif what == "va":
                        take(vat, src[:, :])
                    elif what == "va_t":
                        take(V[:, :, 0:P], src[:, :].rearrange("p (a b) -> p a b", b=P))
                    elif what == "qa":
                        take(qa[:, i, 0:nq], scale=HD ** -0.5)
                    elif what == "qn":
                        if i == 0:
                            act.wait_ge(ob_split, 4 * (l + 1))
                        take(qn[:, i, 0:nq], scale=HD ** -0.5)
                    elif what == "kn":
                        take(kn[:, i, :], src[:, :])
                    elif what == "vn":
                        s, tp = i
                        take(V[:, 2 * tp:2 * tp + 2, P + 256 * s:P + 256 * s + 256],
                             src[:, :].rearrange("p (a b) -> p a b", b=256))
                    elif what == "ux":
                        if i >= 2:
                            wait_taken(act, step_of[l, "gc", i - 2])
                        take(gt[:, i % 2, 0:nq])
                    elif what == "gx":
                        r, n = i
                        if n >= 2 or r:
                            wait_taken(act, step_of[l, "br", (r, n - 2) if n >= 2 else (r - 1, n + 6)])
                        take(gt[:, n % 2, 0:nq], func=ACT.Tanh, scale=0.5, bias=bgh[:, 8 * r + n:8 * r + n + 1])
                    elif what == "wout":
                        act.wait_ge(tile_done, row["t"])
                        if i == 0 and l == 0:
                            act.wait_ge(m_split, 8)
                            act.dma_start(xm[:], a["x_both"]).then_inc(x_back, 16)
                        square(src[:, 0:nq], nn, i, nq)
                        act.activation(y[:, i, 0:nq], src[:, 0:nq], ACT.Copy).then_inc(taken[bank], 1)
                norm_root(nn, nq)

            def ffn():
                for h in range(2):
                    u0, t0, nF = 2 * g_gu[h], t_gu[h], F_HALF[h]
                    split_to(u0 + 1)
                    n = nF // 2
                    nxt[0] = u0 + 4 * (n - 1) + 2

                    def body(i, last):
                        for s in range(2):
                            stage_ahead(u0, None, t0, 1024, i, s, last)
                            act.wait_ge(tile_done, t0 + 4 * i + 2 * s + 1)
                            act.activation(gt[:, s, :], S[s][:, :], ACT.Tanh, scale=0.5).then_inc(tanh_done, 1)
                    body.own_per = 0
                    loop(act, n, body)
                    u0, t0 = 2 * g_dn[h], t_dn[h]
                    w = nF * P // 2
                    if h == 0:
                        split_to(u0 + 1)
                        n = DN_STAGE // 2
                        nxt[0] = u0 + 4 * (n - 1) + 2

                        def body(i, last):
                            for s in range(2):
                                stage_ahead(u0, None, t0, w, i, s, last)
                                act.wait_ge(tile_done, t0 + 4 * i + 2 * s + 2)
                                act.activation(y[:, bass.ds(2 * i + s, 1), :], pp[s][:, :].rearrange("p (a b) -> p a b", a=1),
                                               ACT.Copy).then_inc(taken[s], 1)
                        body.own_per = 0
                        loop(act, n, body)
                    else:
                        for n in range(KT):
                            split_to(u0 + 2 * n + 3)
                            act.wait_ge(taken[n % 2], use_dn[1] + n // 2 + 1)
                            square(y[:, n, :], 3, n, TOK)
                norm_root(3, TOK)

            ada(0)
            prenorm(0, 0, 0, TOK, (0, 0))
            mixer(0, 1, None)
            prenorm(2, 0, 1, TOK, (0, 1))
            ffn()
            ada(1)
            prenorm(4, 1, 0, TOK, (1, 2))
            mixer(1, 5, None)
            wait_taken(act, step_of[1, "rope_q", 3])
            act.dma_start(ctab[:], a["routing"]).then_inc(rc_in, 16)
            prenorm(6, 1, 1, SEQ, (2, 3))

            for n in range(4):
                act.wait_ge(rt_pe, n + 1)
                act.activation(ht[:, n // 2, 512 * (n % 2):512 * (n % 2) + 512], [pp[0], pp[1], S[0], S[1]][n][:, :],
                               ACT.Copy).then_inc(ht_copied, 1)
            act.wait_ge(rt_dve, 1)
            act.activation(rt[:, 8:10], rt[:, 10:12], ACT.Exp).then_inc(rt_act, 1)
            act.wait_ge(routed, 1)
            n_jobs = act.value_load(jobs[0:1, 12:13], min_val=1, max_val=MAX_JOBS)
            with act.Fori(0, n_jobs) as j:
                def hi(i):
                    act.wait_ge(e_raw[i % RAW_E], j * (16 * JOB_SLABS // RAW_E) + 16 * (i // RAW_E + 1))
                    act.wait_ge(e_used, j * JOB_SLABS + (i + 1))
                    act.activation(wse[i % SPLIT_E][:, 0, :, :], raw_e[i % RAW_E], ACT.Copy).then_inc(e_hi, 1)

                def hT_hi(q):
                    act.wait_ge(e_T, j * GU_GROUPS + (q + 1))
                    act.activation(hT[0][:, 2 * q:2 * q + 2, :], T[q % 2][:, 0:256].rearrange("p (a b) -> p a b", b=P),
                                   ACT.Copy).then_inc(e_hThi, 1)

                hi(0)
                act.wait_ge(e_gath, 2 * j + 1)
                for n in range(2):
                    act.activation(xg[0][:, 4 * n:4 * n + 4, :], pp[n][:, :].rearrange("p (a b) -> p a b", b=P),
                                   ACT.Copy).then_inc(e_xghi, 1)
                act.wait_ge(e_gath, 2 * j + 2)
                act.activation(ohT, T[1][:, 0:SEQ], ACT.Copy).then_inc(e_ohT, 1)
                hi(1)
                for q in range(GU_GROUPS):
                    hi(2 * q + 2)
                    hi(2 * q + 3)
                    act.wait_ge(e_used, j * JOB_SLABS + (2 * q + 2 + SPLIT_E))
                    act.activation(tge[:, q % 2, :], S[q % 2][:, 0:256], ACT.Tanh, scale=0.5).then_inc(e_tanh, 1)
                    if q:
                        hT_hi(q - 1)
                for d in range(DN_SLABS):
                    if GU_SLABS + d + 2 < JOB_SLABS:
                        hi(GU_SLABS + d + 2)
                    if d == 0:
                        hT_hi(GU_GROUPS - 1)
                act.wait_ge(e_used, j * JOB_SLABS + (JOB_SLABS + SPLIT_E))
                for n in range(2):
                    act.activation(yb[:, 512 * n:512 * n + 512], O[n][:, :], ACT.Copy).then_inc(e_yb, 1)
            act.wait_ge(e_acc, n_jobs * 4 + 1)
            for k in range(KT):
                square(yacc[:, k, :], 7, k, SEQ)
            norm_root(7, SEQ)

        @block.vector
        def _(dve):
            own = Own(dve, dve_self)
            nxt = [0]

            def split_lo(hval, slot, half, w):
                dve.wait_ge(hi_done, hval)
                dve.tensor_tensor(wsp[:, slot, 1, 0:w], raw[:, slot // 2, half * w:half * w + w],
                                  wsp[:, slot, 0, 0:w], ALU.subtract).then_inc(lo_done, 1)

            def split_to(u):
                while nxt[0] <= u and nxt[0] < N_UNITS:
                    n = nxt[0]
                    split_lo(n + 1, n % 4, n % 2, width[n])
                    nxt[0] += 1

            def stage_ahead(u0, w, i, s, last):
                if last and s == 1:
                    split_to(nxt[0] + 1)
                    return
                for h in range(2):
                    ur = 2 * (s + 1) + h
                    split_lo(u0 + ur + 1 + 4 * i, (u0 + ur) % 4, h, w)
                if last:
                    nxt[0] += 2

            dve.memset(rt[0:1, 0:1], 0.0).then_inc(gu_taken, 2)
            dve.wait_ge(c_ready, 1)
            own.link(dve.scalar_tensor_tensor(cf[:], cf[:], 1.0, cc[:], ALU.add, ALU.mult))
            own.link(dve.tensor_scalar(c4[:, :, 0:2], cf[:], 0.5, None, ALU.mult))
            dve.scalar_tensor_tensor(c4[:, :, 2:4], cf[:], 0.5, c4[:, :, 0:2], ALU.mult, ALU.subtract).then_inc(c_ready, 1)

            def ada(l):
                u0 = 2 * g_ada[l]
                split_to(u0 + 1)
                n = ADA_SLABS // 2
                nxt[0] = u0 + 4 * (n - 1) + 2

                def body(i, last):
                    for s in range(2):
                        stage_ahead(u0, 1024, i, s, last)
                body.own_per = 0
                loop(dve, n, body)
                dve.wait_ge(cols_done, ADA_SLABS * (l + 1))
                b = vec[:, l, V_BADA:V_BADA + 48].rearrange("p (a c) -> p a c", c=1).to_broadcast([P, 48, 2])
                own.link(dve.tensor_tensor(mod[:].rearrange("p a b c -> p (a b) c"),
                                           T[0][:, 0:96].rearrange("p (a c) -> p a c", c=2), b, ALU.add))
                for which, (gpre, gpost) in enumerate(((V_GPRE, V_GPOST), (V_GPREF, V_GPOSTF))):
                    gv = [vec[:, l, v:v + 8].rearrange("p (a c) -> p a c", c=1).to_broadcast([P, 8, 2]) for v in (gpre, gpost)]
                    own.link(dve.scalar_tensor_tensor(am[:, 2 * which], mod[:, 3 * which + 1], 1.0, gv[0], ALU.add, ALU.mult))
                    own.link(dve.tensor_tensor(am[:, 2 * which + 1], mod[:, 3 * which + 2], gv[1], ALU.mult))
                dve.tensor_scalar(bgh[:], vec[:, l, V_BGATE:V_BGATE + 24], 0.5, None, ALU.mult).then_inc(mod_ready, 1)

            def prenorm(n, l, which, N, hs):
                dve.wait_ge(sd_done, n + 1)
                own.link(dve.reciprocal(rs[:, 0:N], sd[:, 0:N]))
                for k in range(KT + 1):
                    if k < KT:
                        if k >= 2:
                            dve.wait_ge(affine, aff[0] + (k - 1) * (N // SEQ))
                        dve.tensor_tensor(gt[:, k % 2, 0:N], xm[:, k, 0:N], rs[:, 0:N], ALU.mult).then_inc(scaled, 1)
                    if k >= 1:
                        dve.wait_ge(affine, aff[0] + k * (N // SEQ))
                        v = hfa[:, k - 1, :] if which == 1 and l == 1 else hf2[:, (k - 1) % 2, 0:N]
                        own.link(dve.tensor_copy(hx[:, 0, k - 1, 0:N], v))
                        dve.tensor_tensor(hx[:, 1, k - 1, 0:N], v, hx[:, 0, k - 1, 0:N], ALU.subtract).then_inc(h_split, 1)
                aff[0] += KT * (N // SEQ)

            aff = [0]

            def postnorm(n, l, which, N, src):
                dve.wait_ge(sd_done, n + 1)
                own.link(dve.reciprocal(rs[:, 0:N], sd[:, 0:N]))
                if n == 1:
                    dve.wait_ge(x_back, 16)
                for k in range(KT):
                    if k >= 2:
                        dve.wait_ge(x_upd, 8 * pm[0] + k - 1)
                    own.link(dve.tensor_tensor(gt[:, k % 2, 0:N], src[:, k, 0:N], rs[:, 0:N], ALU.mult))
                    for s in range(N // SEQ):
                        c = slice(SEQ * s, SEQ * s + SEQ)
                        ins = dve.scalar_tensor_tensor(xm[:, k, c], gt[:, k % 2, c], am[:, 2 * which + 1, k, s:s + 1],
                                                       xm[:, k, c], ALU.mult, ALU.add)
                        if s == N // SEQ - 1:
                            ins.then_inc(x_upd, 1)
                        else:
                            own.link(ins)
                pm[0] += 1

            pm = [0]

            def attn(l, b, s):
                units = attn_units(l)
                nqt = (TOK if l == 0 else SEQ) // P
                if s < len(units):
                    tt, half, qt = units[s]
                    w = unit_base[l, b] + s
                    n = TOK if qt < 2 else SEQ
                    sc = st[:, w % 4, :]
                    bank = S[w % 2]
                    dve.wait_ge(scores_done, w + 1)
                    if qt < 2:
                        if b == 0:
                            c = slice(P, 2 * P) if qt == 0 else slice(0, P)
                            own.link(dve.tensor_tensor(bank[:, c], bank[:, c], wmask[:, qt, :], ALU.add))
                        else:
                            dve.wait_ge(bias_ready, head_base[l, b] + 2 * tt + half + 1)
                            own.link(dve.tensor_tensor(bank[:, 0:SEQ], bank[:, 0:SEQ], bias[:, half, qt, :], ALU.add))
                    own.link(dve.reduce_max(sc[:, 0:1], bank[:, 0:n], AX.X))
                    if b == 0:
                        head = tt + 4 * half
                        dve.tensor_scalar(sc[:, 1:2], sc[:, 0:1], vec[:, l, V_SINK + head:V_SINK + head + 1], -1.0,
                                          ALU.max, ALU.mult).then_inc(pre_done, 1)
                    else:
                        dve.tensor_scalar(sc[:, 1:2], sc[:, 0:1], -1.0, None, ALU.mult).then_inc(pre_done, 1)
                if 0 <= s - 1 < len(units):
                    w = unit_base[l, b] + s - 1
                    n = TOK if units[s - 1][2] < 2 else SEQ
                    sc = st[:, w % 4, :]
                    dve.wait_ge(exp_done, w + 1)
                    if b == 0:
                        own.link(dve.tensor_tensor(sc[:, 2:3], sc[:, 2:3], sc[:, 3:4], ALU.add))
                    own.link(dve.reciprocal(sc[:, 4:5], sc[:, 2:3]))
                    dve.tensor_scalar(pr[:, w % 2, 0:n], pr[:, w % 2, 0:n], sc[:, 4:5], None, ALU.mult).then_inc(probs_done, 1)
                if 0 <= s - 4 < len(units) and (s - 4) % (2 * nqt) == 2 * nqt - 1:
                    tt = units[s - 4][0]
                    ot = otile_base[l, b] + tt
                    dve.wait_ge(o_hi, ot + 1)
                    dve.tensor_tensor(o_br[2 * b][:, 1, tt, 0:nqt * P], O[ot % 2][:, 0:nqt * P],
                                      o_br[2 * b][:, 0, tt, 0:nqt * P], ALU.subtract).then_inc(o_split, 1)

            tmp_read = [None]

            def mixer(l):
                nq = TOK if l == 0 else SEQ
                mg = xm if l == 0 else xm[:, :, SEQ:TOK]
                for row in mixer_steps[l]:
                    for b, s in row["slots"]:
                        attn(l, b, s)
                    what, i, u, bank = row["what"], row["i"], row["u"], row["bank"]
                    if u is not None:
                        split_to(u + 2 + (what == "vn"))
                    src = pp[bank]
                    if what in ("rope_q", "rope_k"):
                        v = qa[:, i, 0:SEQ] if what == "rope_q" else ka[:, 0:SEQ]
                        dve.wait_ge(tile_done, row["t"])
                        if tmp_read[0] is not None:
                            wait_taken(dve, tmp_read[0])
                        tmp_read[0] = row
                        own.link(dve.tensor_tensor(tmp[:, 0:SEQ], src[:, 0:SEQ], ctab[:, 1, :], ALU.mult))
                        own.link(dve.tensor_tensor(v, v, ctab[:, 0, :], ALU.mult))
                        dve.tensor_tensor(v, v, tmp[:, 0:SEQ], ALU.add).then_inc(taken[bank], 1)
                    elif what == "gc":
                        dve.wait_ge(tile_done, row["t"])
                        wait_taken(dve, step_of[l, "ux", i])
                        if 4 * l + i >= 2:
                            dve.wait_ge(conv_done, 4 * l + i - 1)
                        dve.tensor_tensor(cu[:, i % 2, 0:nq], src[:, 0:nq], gt[:, i % 2, 0:nq], ALU.mult).then_inc(taken[bank], 1)
                    elif what == "gb":
                        dve.wait_ge(tile_done, row["t"])
                        dve.wait_ge(conv_done, 4 * l + i + 1)
                        if i >= 2:
                            dve.wait_ge(ob_split, 4 * l + i - 1)
                        dve.tensor_tensor(ob[:, i % 2, 0:nq], src[:, 0:nq], cv[:, i, 0:nq], ALU.mult).then_inc(taken[bank], 1)
                        wait_taken(dve, row)
                        own.link(dve.tensor_copy(o_br[1][:, 0, i, 0:nq], ob[:, i % 2, 0:nq]))
                        dve.tensor_tensor(o_br[1][:, 1, i, 0:nq], ob[:, i % 2, 0:nq], o_br[1][:, 0, i, 0:nq],
                                          ALU.subtract).then_inc(ob_split, 1)
                    elif what == "br":
                        r, n = i
                        dve.wait_ge(tile_done, row["t"])
                        wait_taken(dve, step_of[l, "gx", i])
                        dst = mg[:, n, 0:nq] if r == 0 else tmp[:, 0:nq]
                        if tmp_read[0] is not None:
                            wait_taken(dve, tmp_read[0])
                            tmp_read[0] = None
                        dve.scalar_tensor_tensor(dst, gt[:, n % 2, 0:nq], 1.0, src[:, 0:nq], ALU.add, ALU.mult
                                                 ).then_inc(taken[bank], 1)
                        wait_taken(dve, row)
                        if r:
                            own.link(dve.tensor_tensor(mg[:, n, 0:nq], mg[:, n, 0:nq], tmp[:, 0:nq], ALU.add))
                        if r == 2:
                            own.link(dve.tensor_scalar(m_sp[:, 0, n, 0:nq], mg[:, n, 0:nq], 0.5, None, ALU.mult))
                            dve.scalar_tensor_tensor(m_sp[:, 1, n, 0:nq], mg[:, n, 0:nq], 0.5, m_sp[:, 0, n, 0:nq],
                                                     ALU.mult, ALU.subtract).then_inc(m_split, 1)

            def ffn():
                for h in range(2):
                    u0, t0, nF = 2 * g_gu[h], t_gu[h], F_HALF[h]
                    split_to(u0 + 1)
                    n = nF // 2
                    nxt[0] = u0 + 4 * (n - 1) + 2
                    f0 = h * F_HALF[0]

                    def body(i, last):
                        for s in range(2):
                            stage_ahead(u0, 1024, i, s, last)
                            dve.wait_ge(tile_done, t0 + 4 * i + 2 * s + 2)
                            dve.wait_ge(tanh_done, f0 + 2 * i + s + 1)
                            own.link(dve.scalar_tensor_tensor(gt[:, s, :], gt[:, s, :], 1.0, S[s][:, :], ALU.add, ALU.mult))
                            dve.scalar_tensor_tensor(hf2[:, s, :], gt[:, s, :], 0.5, T[s][:, :], ALU.mult, ALU.mult
                                                     ).then_inc(gu_taken, 1)
                            dve.wait_ge(gu_taken, f0 + 2 * i + s + 3)
                            f = bass.ds(2 * i + s, 1)
                            hv = hf2[:, s, :].rearrange("p (a b) -> p a b", a=1)
                            own.link(dve.tensor_copy(hF[:, 0, f, :], hv))
                            dve.tensor_tensor(hF[:, 1, f, :], hv, hF[:, 0, f, :], ALU.subtract).then_inc(hF_done, 1)
                            dve.wait_ge(hF_done, f0 + 2 * i + s + 1)
                    body.own_per = 4
                    loop(dve, n, body, own)
                    u0 = 2 * g_dn[h]
                    w = nF * P // 2
                    if h == 0:
                        split_to(u0 + 1)
                        n = DN_STAGE // 2
                        nxt[0] = u0 + 4 * (n - 1) + 2

                        def body(i, last):
                            for s in range(2):
                                stage_ahead(u0, w, i, s, last)
                        body.own_per = 0
                        loop(dve, n, body)
                    else:
                        for n in range(KT):
                            split_to(u0 + 2 * n + 3)
                            dve.wait_ge(tile_done, t_dn[1] + 2 * n + 2)
                            dve.tensor_tensor(y[:, n, :], pp[n % 2][:, :], y[:, n, :], ALU.add).then_inc(taken[n % 2], 1)

            ada(0)
            prenorm(0, 0, 0, TOK, 0)
            mixer(0)
            postnorm(1, 0, 0, TOK, y)
            prenorm(2, 0, 1, TOK, 1)
            ffn()
            postnorm(3, 0, 1, TOK, y)
            ada(1)
            prenorm(4, 1, 0, TOK, 2)
            mixer(1)
            postnorm(5, 1, 0, SEQ, y)
            prenorm(6, 1, 1, SEQ, 3)

            L = rt[:, 16:32].rearrange("p (a b) -> p a b", b=NE)
            O1 = rt[:, 32:48].rearrange("p (a b) -> p a b", b=NE)
            O2 = rt[:, 48:64].rearrange("p (a b) -> p a b", b=NE)
            X1 = rt[:, 64:80].rearrange("p (a b) -> p a b", b=NE)
            AS = rt[:, 80:96].rearrange("p (a b) -> p a b", b=NE)
            mx = rt[:, 12:16]
            ix = rt[:, 96:98]
            cn, nb, ea, eb = rt[:, 104:112], rt[:, 112:120], rt[:, 120:128], rt[:, 128:136]

            def b8(v):
                return v.rearrange("p (a c) -> p a c", c=1).to_broadcast([P, 2, NE])

            def c8(v):
                return v.rearrange("p (a c) -> p a c", a=1).to_broadcast([P, 2, NE])

            dve.wait_ge(rt_pe, 5)
            dve.wait_ge(rc_in, 16)
            own.link(dve.tensor_tensor(L, O[0][:, 0:16].rearrange("p (a b) -> p a b", b=NE), c8(br[:]), ALU.add))
            for n, o in enumerate((O1, O2)):
                own.link(dve.tensor_reduce(mx[:, 2 * n:2 * n + 2], L, AX.X, ALU.max))
                own.link(dve.tensor_tensor(X1, L, b8(mx[:, 2 * n:2 * n + 2]), ALU.is_equal))
                own.link(dve.scalar_tensor_tensor(X1, X1, -99.0, c8(iota8b), ALU.mult, ALU.add))
                own.link(dve.tensor_reduce(ix, X1, AX.X, ALU.min))
                own.link(dve.tensor_tensor(o, c8(iota8), b8(ix), ALU.is_equal))
                if n == 0:
                    own.link(dve.scalar_tensor_tensor(L, o, -BIG, L, ALU.mult, ALU.add))
            dve.tensor_tensor(rt[:, 10:12], mx[:, 2:4], mx[:, 0:2], ALU.subtract).then_inc(rt_dve, 1)
            dve.tensor_tensor(AS, O1, O2, ALU.add).then_inc(rt_dve, 1)
            dve.wait_ge(rt_act, 1)
            own.link(dve.tensor_scalar(rt[:, 98:100], rt[:, 8:10], 1.0, None, ALU.add))
            own.link(dve.reciprocal(rt[:, 4:6], rt[:, 98:100]))
            own.link(dve.tensor_tensor(rt[:, 6:8], rt[:, 4:6], rt[:, 8:10], ALU.mult))
            dve.wait_ge(rt_pe, 6)
            own.link(dve.tensor_copy(cn, O[0][:, 48:56]))
            own.link(dve.tensor_scalar(nb, cn, 0.5, None, ALU.is_ge))
            own.link(dve.tensor_scalar(ea, cn, P + 0.5, None, ALU.is_ge))
            own.link(dve.tensor_tensor(nb, nb, ea, ALU.add))
            src, dst = nb, ea
            for sh in (1, 2, 4):
                own.link(dve.tensor_copy(dst[:, 0:sh], src[:, 0:sh]))
                own.link(dve.tensor_tensor(dst[:, sh:8], src[:, sh:8], src[:, 0:8 - sh], ALU.add))
                src, dst = dst, (eb if dst is ea else ea)
            end, beg = src, rt[:, 136:144]
            own.link(dve.tensor_tensor(beg, end, nb, ALU.subtract))
            own.link(dve.scalar_tensor_tensor(AS, c8(beg), float(P), O[0][:, 32:48].rearrange("p (a b) -> p a b", b=NE),
                                              ALU.mult, ALU.add))
            for n, o in enumerate((O1, O2)):
                own.link(dve.tensor_tensor(X1, AS, o, ALU.mult))
                own.link(dve.reduce_sum(rt[:, 2 * n:2 * n + 2], X1, AX.X))
            cmp = rt[0:1, 256:256 + 96].rearrange("p (a b) -> p a b", b=NE)
            own.link(dve.tensor_tensor(cmp, iotaj.rearrange("p (a c) -> p a c", c=1).to_broadcast([1, 12, NE]),
                                       end[0:1, :].rearrange("p (a c) -> p a c", a=1).to_broadcast([1, 12, NE]), ALU.is_ge))
            own.link(dve.reduce_sum(rt[0:1, 144:156], cmp, AX.X))
            own.link(dve.tensor_scalar(jobs[0:1, 0:12], rt[0:1, 144:156], float(NE - 1), None, ALU.min))
            own.link(dve.tensor_copy(jobs[0:1, 12:13], end[0:1, 7:8]))
            dve.wait_ge(ht_copied, 4)
            own.link(dve.memset(rt[0:1, 160:161], 0.0))
            dve.memset(rt[0:1, 161:162], 0.0).then_inc(e_lo, RAW_E)
            dve.memset(rt[0:1, 164:165], 0.0).then_inc(e_acc, 1)
            dve.memset(rt[0:1, 162:163], 0.0).then_inc(routed, 1)
            dve.wait_ge(routed, 1)
            n_jobs = dve.value_load(jobs[0:1, 12:13], min_val=1, max_val=MAX_JOBS)

            def one_hot():
                pos, gate = rt[:, 0:4], rt[:, 4:8]
                for n in range(2):
                    own.mark(dve.tensor_scalar(oh[:, n, :], iota, pos[:, n:n + 1], None, ALU.is_equal))
                    own.mark(dve.tensor_scalar(ohg[:, n, :], iota, pos[:, n:n + 1], gate[:, n:n + 1], ALU.is_equal, ALU.mult))
                    own.link(dve.tensor_scalar(oh2[:, n, :], iota, pos[:, 2 + n:3 + n], None, ALU.is_equal))
                own.mark(dve.tensor_tensor(oh, oh, oh2, ALU.add))
                for n in range(2):
                    own.mark(dve.scalar_tensor_tensor(ohg[:, n, :], oh2[:, n, :], gate[:, 2 + n:3 + n], ohg[:, n, :],
                                                      ALU.mult, ALU.add))
                own.link(dve.tensor_scalar(pos, pos, -float(P), None, ALU.add))
                dve.memset(rt[0:1, 163:164], 0.0).then_inc(e_onehot, 1)
                dve.wait_ge(e_onehot, own.jobs_done + 1)

            own.jobs_done = 0
            one_hot()
            own.base, own.k = own.base + own.k, 0
            start = own.base
            dve.wait_ge(yacc_zero, 1)
            with dve.Fori(0, n_jobs) as j:
                own.base, own.jobs_done = start + j * (GU_GROUPS + 10), j + 1

                def lo(i):
                    dve.wait_ge(e_hi, j * JOB_SLABS + (i + 1))
                    w = wse[i % SPLIT_E]
                    dve.tensor_tensor(w[:, 1, :, :], raw_e[i % RAW_E], w[:, 0, :, :], ALU.subtract).then_inc(e_lo, 1)

                def hT_lo(q):
                    dve.wait_ge(e_hThi, j * GU_GROUPS + (q + 1))
                    dve.tensor_tensor(hT[1][:, 2 * q:2 * q + 2, :], T[q % 2][:, 0:256].rearrange("p (a b) -> p a b", b=P),
                                      hT[0][:, 2 * q:2 * q + 2, :], ALU.subtract).then_inc(e_hT, 1)

                lo(0)
                for n in range(2):
                    dve.wait_ge(e_xghi, 2 * j + (n + 1))
                    dve.tensor_tensor(xg[1][:, 4 * n:4 * n + 4, :], pp[n][:, :].rearrange("p (a b) -> p a b", b=P),
                                      xg[0][:, 4 * n:4 * n + 4, :], ALU.subtract).then_inc(e_xg, 1)
                lo(1)
                for q in range(GU_GROUPS):
                    lo(2 * q + 2)
                    lo(2 * q + 3)
                    dve.wait_ge(e_tanh, j * GU_GROUPS + (q + 1))
                    own.link(dve.scalar_tensor_tensor(tge[:, q % 2, :], tge[:, q % 2, :], 1.0, S[q % 2][:, 0:256],
                                                      ALU.add, ALU.mult))
                    dve.scalar_tensor_tensor(hse[:, q % 2, :], tge[:, q % 2, :], 0.5, S[q % 2][:, 256:512],
                                             ALU.mult, ALU.mult).then_inc(e_h, 1)
                    if q:
                        hT_lo(q - 1)
                for d in range(DN_SLABS):
                    if GU_SLABS + d + 2 < JOB_SLABS:
                        lo(GU_SLABS + d + 2)
                    if d == 0:
                        hT_lo(GU_GROUPS - 1)
                one_hot()
                assert own.k == GU_GROUPS + 10
                for n in range(4):
                    dve.wait_ge(e_scat, 4 * j + (n + 1))
                    v = yacc[:, 2 * n:2 * n + 2, :]
                    dve.tensor_tensor(v, [S[0], S[1], T[0], T[1]][n][:, :].rearrange("p (a b) -> p a b", b=SEQ), v,
                                      ALU.add).then_inc(e_acc, 1)
            own.base, own.k = start + n_jobs * (GU_GROUPS + 10), 0
            postnorm(7, 1, 1, SEQ, yacc)

        @block.tensor
        def _(pe):
            mm = pe.matmul

            def split_mm(dst, w_hi, w_lo, x_hi, x_lo, first, last):
                mm(dst, w_hi, x_hi, start=first, stop=False)
                mm(dst, w_hi, x_lo, start=False, stop=False)
                return mm(dst, w_lo, x_hi, start=False, stop=last)

            def norm_sum(n, k, N):
                pe.wait_ge(sq_done, 8 * n + k + 1)
                mm(O[1][:, 0:N], mean[:], sq[:, k % 2, 0:N], start=(k == 0), stop=(k == KT - 1)).then_inc(sum_done, 1)

            def ada(l):
                u0, t0, use0 = 2 * g_ada[l], t_ada[l], use_ada[l]

                def body(i, last):
                    for s in range(2):
                        for h in range(2):
                            pe.wait_ge(lo_done, u0 + 4 * i + 2 * s + h + 1)
                            if h == 0 and not (isinstance(i, int) and use0 + i == 0):
                                pe.wait_ge(taken[s], use0 + i)
                            slot = (u0 + 2 * s + h) % 4
                            for k in range(4):
                                for part in range(2):
                                    ins = mm(pp[s][0:4, 0:256], c4[:, 4 * h + k, :], wsp[:, slot, part, 256 * k:256 * k + 256],
                                             start=(h + k + part == 0), stop=(h == 1 and k == 3 and part == 1))
                            ins.then_inc(tile_done, 1)
                    for s in range(2):
                        pe.wait_ge(taken[s], use0 + i + 1)
                        for h in range(2):
                            c = 8 * i + 4 * s + 2 * h
                            dst = T[0][:, bass.ds(c, 2)]
                            ins = mm(dst, adr[:, s, P * h:P * h + P], sel[:], start=True, stop=True)
                        ins.then_inc(cols_done, 1)
                body.own_per = 0
                loop(pe, ADA_SLABS // 2, body, first=(l == 0))

            def attn(l, b, s):
                units = attn_units(l)
                nqt = (TOK if l == 0 else SEQ) // P
                base = unit_base[l, b]
                if s < len(units):
                    tt, half, qt = units[s]
                    w = base + s
                    pe.wait_ge(q2_ready, w + 1)
                    if w >= 2:
                        pe.wait_ge(exp_done, w - 1)
                    if b == 0:
                        wait_taken(pe, step_of[l, "rope_k", 0])
                        keys = ka
                    else:
                        wait_taken(pe, step_of[l, "kn", tt])
                        keys = kn[:, tt, :]
                    k0 = 0 if qt < 2 else SEQ
                    mm(S[w % 2][:, 0:TOK - k0], q2[:, half, w % 2, :], keys[:, k0:TOK], start=True, stop=True
                       ).then_inc(scores_done, 1)
                if 0 <= s - 2 < len(units):
                    w = base + s - 2
                    kts = 4 if units[s - 2][2] < 2 else 2
                    pe.wait_ge(probs_done, w + 1)
                    if w >= 2:
                        pe.wait_ge(pT_copied, w - 1)
                    for k in range(kts):
                        ins = pe.transpose(T[w % 2][:, P * k:P * k + P], pr[:, w % 2, P * k:P * k + P], ident[:])
                    ins.then_inc(pT_done, 1)
                if 0 <= s - 3 < len(units):
                    w = base + s - 3
                    tt, half, qt = units[s - 3]
                    kts = range(4) if qt < 2 else range(2, 4)
                    ot = otile_base[l, b] + tt
                    pe.wait_ge(pT_copied, w + 1)
                    if half == 0 and qt == 0 and ot >= 2:
                        pe.wait_ge(o_split, ot - 1)
                    if s - 3 == 0:
                        if b == 0:
                            wait_taken(pe, step_of[l, "va_t", 0])
                        else:
                            for key in ((0, 0), (0, 1), (1, 0), (1, 1)):
                                wait_taken(pe, step_of[l, "vn", key])
                    vc = HD * half if b == 0 else P + HD * (2 * tt + half)
                    for n, k in enumerate(kts):
                        ins = mm(O[ot % 2][HD * half:HD * half + HD, P * qt:P * qt + P], V[:, k, vc:vc + HD],
                                 prT[:, w % 2, n, :], start=(n == 0), stop=(n == len(kts) - 1))
                    ins.then_inc(pv_done, 1)

            def mixer(l, nn, hs):
                nq = TOK if l == 0 else SEQ
                pe.wait_ge(h_split, 8 * (hs + 1))
                for row in mixer_steps[l]:
                    for b, s in row["slots"]:
                        attn(l, b, s)
                    what, i, u, bank = row["what"], row["i"], row["u"], row["bank"]
                    dst = pp[bank]
                    if row["use"] > 1:
                        pe.wait_ge(taken[bank], row["use"] - 1)
                    if u is not None:
                        pe.wait_ge(lo_done, u + 1 + (what == "vn"))
                        slot = u % 4
                    if what in ("rope_q", "rope_k"):
                        wait_taken(pe, step_of[l, "qa" if what == "rope_q" else "ka", i])
                        v = qa[:, i, 0:SEQ] if what == "rope_q" else ka[:, 0:SEQ]
                        if i == 0:
                            pe.wait_ge(consts_in, 16 * 7)
                        ins = mm(dst[:, 0:SEQ], rot[:], v, start=True, stop=True)
                    elif what == "va_t":
                        wait_taken(pe, step_of[l, "va", 0])
                        for k in range(4):
                            ins = pe.transpose(dst[:, P * k:P * k + P], vat[:, P * k:P * k + P], ident[:])
                    elif what == "vn":
                        s, tp = i
                        for q in range(2):
                            tk = slice(P * (2 * tp + q), P * (2 * tp + q) + P)
                            d = dst[:, 256 * q:256 * q + 256]
                            for k in range(KT):
                                sl = (u + k // 4) % 4
                                wh, wl = (wsp[:, sl, part, 256 * (k % 4):256 * (k % 4) + 256] for part in range(2))
                                mm(d, hx[:, 0, k, tk], wh, start=(k == 0), stop=False)
                                mm(d, hx[:, 0, k, tk], wl, start=False, stop=False)
                                ins = mm(d, hx[:, 1, k, tk], wh, start=False, stop=(k == KT - 1))
                    else:
                        if what == "br":
                            x, nk = o_br[i[0]], BT
                            if i[1] == 0:
                                if i[0] == 1:
                                    pe.wait_ge(ob_split, 4 * (l + 1))
                                else:
                                    pe.wait_ge(o_split, otile_base[l, i[0] // 2] + 4)
                        elif what == "wout":
                            x, nk = m_sp, KT
                            if i == 0:
                                pe.wait_ge(m_split, 8 * (l + 1))
                        else:
                            x, nk = hx, KT
                        N = TOK if what in ("ka", "va", "kn") else nq
                        for k in range(nk):
                            ins = split_mm(dst[:, 0:N], wsp[:, slot, 0, P * k:P * k + P], wsp[:, slot, 1, P * k:P * k + P],
                                           x[:, 0, k, 0:N], x[:, 1, k, 0:N], k == 0, k == nk - 1)
                    ins.then_inc(tile_done, 1)
                    if what == "wout" and i:
                        norm_sum(nn, i - 1, nq)
                norm_sum(nn, KT - 1, nq)

            def ffn():
                pe.wait_ge(h_split, 16)
                for h in range(2):
                    u0, nF, f0 = 2 * g_gu[h], F_HALF[h], h * F_HALF[0]

                    def body(i, last):
                        for s in range(2):
                            for part, bank in ((0, S[s]), (1, T[s])):
                                pe.wait_ge(lo_done, u0 + 4 * i + 2 * s + part + 1)
                                if part == 0:
                                    pe.wait_ge(gu_taken, f0 + 2 * i + s + 1)
                                slot = (u0 + 2 * s + part) % 4
                                for k in range(KT):
                                    ins = split_mm(bank[:, :], wsp[:, slot, 0, P * k:P * k + P], wsp[:, slot, 1, P * k:P * k + P],
                                                   hx[:, 0, k, :], hx[:, 1, k, :], k == 0, k == KT - 1)
                                ins.then_inc(tile_done, 1)
                    body.own_per = 0
                    loop(pe, nF // 2, body)
                    pe.wait_ge(hF_done, f0 + nF)
                    u0 = 2 * g_dn[h]
                    hk = nF // 2

                    def down(i, s):
                        for part in range(2):
                            pe.wait_ge(lo_done, u0 + 4 * i + 2 * s + part + 1)
                            if part == 0:
                                pe.wait_ge(taken[s], use_dn[h] + i)
                            slot = (u0 + 2 * s + part) % 4
                            for k in range(hk):
                                f = part * hk + k
                                ins = split_mm(pp[s][:, :], wsp[:, slot, 0, P * k:P * k + P], wsp[:, slot, 1, P * k:P * k + P],
                                               hF[:, 0, f, :], hF[:, 1, f, :], f == 0, f == nF - 1)
                            ins.then_inc(tile_done, 1)
                    if h == 0:
                        def body(i, last):
                            down(i, 0)
                            down(i, 1)
                        body.own_per = 0
                        loop(pe, DN_STAGE // 2, body)
                    else:
                        for n in range(KT):
                            down(n // 2, n % 2)
                            if n:
                                norm_sum(3, n - 1, TOK)
                norm_sum(3, KT - 1, TOK)

            pe.wait_ge(c_ready, 2)
            pe.wait_ge(eps_ready, 3)
            ada(0)
            for k in range(KT):
                norm_sum(0, k, TOK)
            mixer(0, 1, 0)
            for k in range(KT):
                norm_sum(2, k, TOK)
            ffn()
            ada(1)
            for k in range(KT):
                norm_sum(4, k, TOK)
            mixer(1, 5, 2)
            for k in range(KT):
                norm_sum(6, k, SEQ)
            pe.wait_ge(h_split, 32)
            for n in range(4):
                for k in range(4):
                    c = 4 * (n % 2) + k
                    ins = pe.transpose([pp[0], pp[1], S[0], S[1]][n][:, P * k:P * k + P],
                                       hfa[:, c, P * (n // 2):P * (n // 2) + P], ident[:])
                ins.then_inc(rt_pe, 1)
            for n in range(2):
                for k in range(KT):
                    ins = mm(O[0][:, NE * n:NE * n + NE], hfa[:, k, P * n:P * n + P], wr[:, k, :], start=(k == 0), stop=(k == KT - 1))
            ins.then_inc(rt_pe, 1)
            pe.wait_ge(rt_dve, 2)
            A0, A1 = rt[:, 80:88], rt[:, 88:96]
            mm(O[0][:, 32:40], tri, A0, start=True, stop=True)
            mm(O[0][:, 40:48], ones, A0, start=True, stop=False)
            mm(O[0][:, 40:48], tri, A1, start=False, stop=True)
            mm(O[0][:, 48:56], ones, A0, start=True, stop=False)
            mm(O[0][:, 48:56], ones, A1, start=False, stop=True).then_inc(rt_pe, 1)
            pe.wait_ge(routed, 1)
            mm(O[0][:, 56:64], ones, A1, start=True, stop=True).then_inc(e_used, SPLIT_E)
            n_jobs = pe.value_load(jobs[0:1, 12:13], min_val=1, max_val=MAX_JOBS)
            with pe.Fori(0, n_jobs) as j:
                def got(i):
                    pe.wait_ge(e_lo, j * JOB_SLABS + (i + 1 + RAW_E))

                def transposes(q):
                    pe.wait_ge(e_h, j * GU_GROUPS + (q + 1))
                    if q >= 2:
                        pe.wait_ge(e_hT, j * GU_GROUPS + (q - 1))
                    for n in range(2):
                        ins = pe.transpose(T[q % 2][:, P * n:P * n + P], hse[:, q % 2, P * n:P * n + P], ident[:])
                    ins.then_inc(e_T, 1)

                pe.wait_ge(e_onehot, j + 1)
                pe.wait_ge(e_acc, 4 * j + 1)
                for k in range(KT):
                    for n in range(2):
                        ins = mm(pp[k // 4][:, P * (k % 4):P * (k % 4) + P], ht[:, n, P * k:P * k + P], oh[:, n, :],
                                 start=(n == 0), stop=(n == 1))
                ins.then_inc(e_gath, 1)
                for n in range(2):
                    ins = pe.transpose(T[1][:, P * n:P * n + P], ohg[:, n, :], ident[:])
                ins.then_inc(e_gath, 1)
                pe.wait_ge(e_xg, 2 * j + 2)
                for q in range(GU_GROUPS):
                    if q >= 2:
                        pe.wait_ge(e_h, j * GU_GROUPS + (q - 1))
                    for h in range(2):
                        i = 2 * q + h
                        got(i)
                        w = wse[i % SPLIT_E]
                        for k in range(4):
                            wh, wl = (w[:, part, 2 * k:2 * k + 2, :] for part in range(2))
                            kk = 4 * h + k
                            d = S[q % 2][:, :].rearrange("p (a b) -> p a b", b=256)
                            mm(d, xg[0][:, kk, :], wh, start=(kk == 0), stop=False)
                            mm(d, xg[0][:, kk, :], wl, start=False, stop=False)
                            ins = mm(d, xg[1][:, kk, :], wh, start=False, stop=(kk == KT - 1))
                        ins.then_inc(e_used, 1)
                    if q == 1:
                        pe.wait_ge(e_ohT, j + 1)
                    if q:
                        transposes(q - 1)
                for d_ in range(DN_SLABS):
                    i = GU_SLABS + d_
                    got(i)
                    if d_ == 0:
                        pe.wait_ge(e_hT, j * GU_GROUPS + 1)
                    pe.wait_ge(e_hT, j * GU_GROUPS + (d_ + 1))
                    w = wse[i % SPLIT_E]
                    for f2 in range(2):
                        f = 2 * d_ + f2
                        for x, part in ((0, 0), (0, 1), (1, 0)):
                            for n in range(2):
                                ins = mm(O[n][:, :].rearrange("p (a b) -> p a b", b=256), hT[x][:, f, :],
                                         w[:, part, 4 * f2 + 2 * n:4 * f2 + 2 * n + 2, :],
                                         start=(f == 0 and x == 0 and part == 0), stop=(f == FE_T - 1 and x == 1))
                    ins.then_inc(e_used, 1)
                    if d_ == 0:
                        transposes(GU_GROUPS - 1)
                for n in range(4):
                    pe.wait_ge(e_yb, 2 * j + (n // 2 + 1))
                    if n == 0:
                        pe.wait_ge(e_hT, (j + 1) * GU_GROUPS)
                    for h in range(2):
                        c = 2 * n + h
                        ins = mm([S[0], S[1], T[0], T[1]][n][:, SEQ * h:SEQ * h + SEQ], yb[:, P * c:P * c + P], ohT,
                                 start=True, stop=True)
                    ins.then_inc(e_scat, 1)
            for k in range(KT):
                norm_sum(7, k, SEQ)


def _tiles(w, cols):
    k = w.shape[0] // P
    return np.stack([w[i * P:(i + 1) * P][:, cols] for i in range(k)], axis=1)


def _pack_dense(inp):
    main, brs = [], []
    qa0, ka0, va0, ux0 = 0, BW, BW + P, BW + 2 * P
    gb0, gc0, qn0, kn0, vn0, gx0 = (ux0 + n * BW for n in range(1, 7))

    def put(*parts):
        main.append(np.concatenate([p.reshape(P, -1) for p in parts], axis=1))

    def ada(l):
        w = inp["w_ada"][l]
        for s in range(ADA_SLABS):
            put(_tiles(w, slice(256 * s, 256 * s + 256)))

    def mixer(l):
        w = inp["w_in"][l]
        col = lambda c0, i: np.arange(c0 + P * i, c0 + P * i + P)
        two = lambda x, y: put(_tiles(w, x), _tiles(w, y))
        qcol = lambda i: np.concatenate([np.arange(qa0 + HD * i, qa0 + HD * i + HD),
                                         np.arange(qa0 + HD * (i + 4), qa0 + HD * (i + 4) + HD)])
        two(col(ka0, 0), col(va0, 0))
        for i in (0, 2):
            two(qcol(i), qcol(i + 1))
        for c in range(BT):
            two(col(ux0, c), col(gc0, c))
        for c0 in (gb0, qn0, kn0):
            for i in (0, 2):
                two(col(c0, i), col(c0, i + 1))
        for s in range(2):
            put(_tiles(w, slice(vn0 + 256 * s, vn0 + 256 * s + 256)))
        for r in range(3):
            wb = inp["w_branch"][l, r]
            if r == 0:
                wb = wb[np.concatenate([np.arange(HD * h, HD * h + HD) for i in range(4) for h in (i, i + 4)])]
            for n in range(0, KT, 2):
                two(col(gx0 + D * r, n), col(gx0 + D * r, n + 1))
                brs.append(np.concatenate([_tiles(wb, slice(P * m, P * m + P)).reshape(P, -1) for m in (n, n + 1)], axis=1))
        wo = inp["w_out"][l]
        for n in range(0, KT, 2):
            put(_tiles(wo, slice(P * n, P * n + P)), _tiles(wo, slice(P * n + P, P * n + 2 * P)))

    ada(0)
    mixer(0)
    gu, dn = inp["w_gu_dense"][0], inp["w_dn_dense"][0]
    dns, f = [], 0
    for nF in F_HALF:
        for j in range(f, f + nF):
            put(_tiles(gu, slice(P * j, P * j + P)), _tiles(gu, slice(FFN_D + P * j, FFN_D + P * j + P)))
        dns.append(np.stack([_tiles(dn[P * f:P * (f + nF)], slice(P * n, P * n + P)).reshape(P, -1) for n in range(KT)]))
        f += nF
    ada(1)
    mixer(1)
    return np.stack(main), np.stack(brs), dns[0], dns[1]


def _pack_experts(inp):
    out = np.empty((NE, JOB_SLABS, P, 8, 256), np.float32)
    gu, dn = inp["w_gu_moe"][0], inp["w_dn_moe"][0]
    for e in range(NE):
        g = gu[e].reshape(2, 4, P, 2, GU_GROUPS, 256)
        out[e, :GU_SLABS] = g.transpose(4, 0, 2, 1, 3, 5).reshape(GU_SLABS, P, 8, 256)
        d = dn[e].reshape(DN_SLABS, 2, P, D)
        out[e, GU_SLABS:] = d.transpose(0, 2, 1, 3).reshape(DN_SLABS, P, 8, 256)
    return out.reshape(NE * JOB_SLABS, P, 8, 256)


def _shape_constants():
    i = np.arange(P)
    rot = np.zeros((P, P), np.float32)
    for m in range(P):
        q = m % 32
        if q < 16:
            rot[m + 16, m] = -1.0
        else:
            rot[m - 16, m] = 1.0
    half = HD // 2
    inv = 1.0 / (10000.0 ** (np.arange(0, half, 2, dtype=np.float32) / np.float32(half)))
    pos = np.arange(SEQ)
    ar = (pos // GRID_W).astype(np.float32)[:, None] * inv[None].astype(np.float32)
    ac = (pos % GRID_W).astype(np.float32)[:, None] * inv[None].astype(np.float32)
    ang = np.concatenate([ar, ar, ac, ac], axis=-1).astype(np.float32)
    cs = np.stack([np.tile(np.cos(ang).T, (2, 1)), np.tile(np.sin(ang).T, (2, 1))], axis=1).astype(np.float32)
    q, k = i[:, None], i[None, :]
    wmask = np.stack([np.where(k + P - q <= WINDOW, 0.0, -BIG), np.where(q + P - k <= WINDOW, 0.0, -BIG)], axis=1)
    c = np.arange(GRID_W)
    start = np.clip(c - NA_COLS // 2, 0, GRID_W - NA_COLS)
    ok = (c[None, :] >= start[:, None]) & (c[None, :] < start[:, None] + NA_COLS)
    cmask = np.tile(np.where(ok, 0.0, -BIG), (2, 1))
    routing = np.zeros((P, 2, SEQ), np.float32)
    routing[:, 0, 0:P] = i[:, None] < i[None, :]
    routing[:, 0, P:2 * P] = 1.0
    routing[:, 1, 0:P] = i[None, :]
    routing[:, 1, P:P + 8] = np.arange(8)
    routing[:, 1, P + 8:P + 16] = np.arange(8) + 99.0
    routing[:, 1, P + 16:P + 28] = np.arange(12)
    return {"ident": np.eye(P, dtype=np.float32), "rot": rot, "cossin": cs, "wmask": wmask.astype(np.float32),
            "cmask": cmask.astype(np.float32), "routing": routing}


def _position_rows(rpb):
    q, k = np.arange(SEQ)[:, None], np.arange(SEQ)[None, :]
    dr = k // GRID_W - q // GRID_W + RPB_R // 2
    dc = np.clip(k % GRID_W - q % GRID_W, 1 - NA_COLS, NA_COLS - 1) + NA_COLS - 1
    return rpb[:, :, dr, dc].reshape(DEPTH, 8, 2, P, SEQ).transpose(0, 1, 3, 2, 4)


def _lay_out(inp):
    col = lambda v: v.reshape(-1, P).T
    vec = []
    for l in range(DEPTH):
        conv = np.concatenate([col(inp["conv_w"][l, k]) for k in range(3)], axis=1)
        vec.append(np.concatenate([col(inp["g_pre_mix"][l]), col(inp["g_post_mix"][l]), col(inp["g_pre_ffn"][l]),
                                   col(inp["g_post_ffn"][l]), col(inp["b_gate"][l]), col(inp["b_ada"][l]), conv,
                                   np.broadcast_to(inp["sink"][l], (P, 8))], axis=1))
    w_main, w_br, w_dn0, w_dn1 = _pack_dense(inp)
    tok = np.concatenate([inp["x"][0], inp["ctx"][0]], axis=0)
    arrays = {
        "w_main": w_main, "w_br": w_br, "w_dn0": w_dn0, "w_dn1": w_dn1, "w_moe": _pack_experts(inp),
        "x_both": tok.T.reshape(KT, P, TOK).transpose(1, 0, 2),
        "c_both": np.stack([inp["c"][0], inp["c_ctx"]], axis=1).reshape(KT, P, 2).transpose(1, 0, 2),
        "vec": np.stack(vec, axis=1), "rpb_rows": _position_rows(inp["rpb"]),
        "w_router": inp["w_router"][0].reshape(KT, P, NE).transpose(1, 0, 2),
        "b_router": np.broadcast_to(inp["b_router"][0], (P, NE)),
    }
    arrays.update(_shape_constants())
    return {k: np.ascontiguousarray(v) for k, v in arrays.items()}


def kernel(**inputs):
    import concourse.bacc as _bacc
    from concourse import mybir as _mybir
    from concourse.bass_utils import run_bass_kernel_spmd as _run

    arrays = _lay_out({k: np.asarray(v) for k, v in inputs.items()})
    nc = _bacc.Bacc("TRN2", target_bir_lowering=False, num_devices=1)
    aps = {k: nc.dram_tensor(f"in_{k}", v.shape, _mybir.dt.from_np(v.dtype), kind="ExternalInput").ap()
           for k, v in arrays.items()}
    out = nc.dram_tensor("out_x", (P, KT, SEQ), _mybir.dt.float32, kind="ExternalOutput").ap()
    build_program(nc, aps, out)
    r = _run(nc, [{f"in_{k}": v for k, v in arrays.items()}], core_ids=[0])
    got = r.results[0]["out_x"]
    return np.ascontiguousarray(got.transpose(2, 1, 0).reshape(1, SEQ, D))
```

```python
import numpy as np
import concourse.bass as bass
from concourse import mybir
from contextlib import ExitStack

F32 = mybir.dt.float32
F32R = mybir.dt.float32r
I32 = mybir.dt.int32
ALU = mybir.AluOpType
ACT = mybir.ActivationFunctionType
AX = mybir.AxisListType

P = 128
D = 1024
KT = D // P
SEQ = 256
TOK = 512
HD = 64
BW = 512
BT = BW // P
DEPTH = 2
WINDOW = 128
GRID_W = 64
NA_COLS = 16
RPB_R, RPB_C = 15, 31
FFN_D = 2816
FFN_E = 3584
NE = 8
EPS = 1e-6
BIG = 1e30

F_HALF = (12, 10)
GU_SLABS = 2 * FFN_E // 256
GU_GROUPS = GU_SLABS // 2
FE_T = FFN_E // P
DN_SLABS = FE_T // 2
JOB_SLABS = GU_SLABS + DN_SLABS
RAW_E, SPLIT_E = 6, 3
MAX_JOBS = 2 * SEQ // P + NE - 1

V_GPRE, V_GPOST, V_GPREF, V_GPOSTF, V_BGATE, V_BADA, V_CONV, V_SINK = 0, 8, 16, 24, 32, 56, 104, 116
V_ALL = 124


def mixer_plan(ada):
    slabs, steps = [], []
    ada = list(ada)

    def slab(array, *tiles):
        slabs.append(array)
        for n, (what, i) in enumerate(tiles):
            steps.append((what, i, 2 * (len(slabs) - 1) + n))

    slab("main", ("ka", 0), ("va", 0))
    steps += [("rope_k", 0, None), ("va_t", 0, None)]
    for i in (0, 2):
        slab("main", ("qa", i), ("qa", i + 1))
        steps += [("rope_q", i, None), ("rope_q", i + 1, None)]
    head = len(steps)

    late = []

    def beside():
        late.clear()
        if ada:
            s = ada.pop(0)
            slabs.append("main")
            steps.append(("ada", s, 2 * (len(slabs) - 1)))
            late.append(("ada_t", s, None))

    def add(array, *tiles):
        slabs.append(array)
        u = 2 * (len(slabs) - 1)
        for n, (what, i) in enumerate(tiles):
            steps.append((what, i, u if what == "vn" else u + n))
            if n == 0:
                steps.extend(late)
                late.clear()

    for c in range(BT):
        add("main", ("ux", c), ("gc", c))
        if c >= 2:
            beside()
    for what in ("gb", "qn", "kn"):
        for i in (0, 2):
            add("main", (what, i), (what, i + 1))
            beside()
    for s in range(2):
        add("main", ("vn", (s, 0)), ("vn", (s, 1)))
    mid = len(steps)
    for r in range(3):
        for n in range(0, KT, 2):
            add("main", ("gx", (r, n)), ("gx", (r, n + 1)))
            add("br", ("br", (r, n)), ("br", (r, n + 1)))
            beside()
        if r == 1:
            end = len(steps)
    for n in range(0, KT, 2):
        slab("main", ("wout", n), ("wout", n + 1))
    return slabs, steps, head, mid, end


ADA_SLABS = 24
ADA_FIRST = 8
ADA_FFN = sum(F_HALF)
ADA_MIXER = [(0, s) for s in range(ADA_FIRST, ADA_SLABS)] + [(1, s) for s in range(ADA_SLABS - ADA_FFN)]
FIRST_NORM = [(), (), (0, 1), (2, 3), (4, 5), (6,), (7,), ()]
ADA_BESIDE_A = 8
PLANS = [mixer_plan(ADA_MIXER), mixer_plan([])]
DN_STAGE = KT


def spread(steps, slots):
    out, done = [], 0
    for n, st in enumerate(steps):
        want = (n + 1) * slots // len(steps)
        out.append((list(range(done, want)), st))
        done = want
    return out


def build_program(nc, a, out):
    ctx = ExitStack()
    with ctx:
        def sb(name, shape, dt=F32):
            return ctx.enter_context(nc.sbuf_tensor(name, shape, dt))

        def sem(name):
            return ctx.enter_context(nc.semaphore(name))

        raw = sb("raw", [P, 2, 2048])
        wsp = sb("wsp", [P, 4, 2, 1024], F32R)
        hx = sb("hx", [P, 2, KT, TOK], F32R)
        opr = sb("opr", [P, 12288], F32R)
        xm = sb("xm", [P, KT, TOK])
        M = sb("M", [P, 14336])

        def view(t, at, *shape):
            n = int(np.prod(shape))
            v = t[:, at:at + n]
            if len(shape) == 2:
                v = v.rearrange("p (a b) -> p a b", b=shape[1])
            if len(shape) == 3:
                v = v.rearrange("p (a b c) -> p a b c", b=shape[1], c=shape[2])
            return v

        o_br = [view(opr, 4096 * r, 2, BT, TOK) for r in range(3)]
        m_sp = view(opr, 0, 2, KT, TOK)
        hF = view(opr, 0, 2, 12, TOK)
        qa = view(M, 0, BT, TOK)
        ka = view(M, 2048, TOK)
        V = view(M, 2560, 4, P + BW)
        qn = view(M, 5120, BT, TOK)
        kn = view(M, 7168, BT, TOK)
        cv = view(M, 5120, BT, TOK)
        cu = view(M, 7168, 2, TOK)
        ob = view(M, 8192, 2, TOK)
        vat = view(M, 8192, TOK)
        y = view(M, 5120, KT, TOK)
        bias = view(M, 9216, 2, 2, 256)
        hf2 = view(M, 9216, 2, TOK)
        pr = view(M, 10240, 2, TOK)
        sq = view(M, 10240, 2, TOK)
        adr_m, adr_f = (M[0:4, c:c + 512].rearrange("p (a b) -> p a b", a=2) for c in (9216, 0))

        def ada_rows(n):
            return (adr_m if n < ADA_BESIDE_A else adr_f)[:, n % 2, :]

        prT = view(M, 11264, 2, 4, P)
        rs = view(M, 11264, TOK)
        sd = view(M, 11776, TOK)
        q2 = view(M, 12288, 2, 2, P)
        gt = view(M, 12800, 2, TOK)
        gt3 = view(M, 12800, 3, TOK)
        tmp = view(M, 13824, TOK)
        hfa = view(M, 0, KT, SEQ)
        yacc = view(M, 0, KT, SEQ)
        ht = view(M, 2048, 2, D)
        yb = view(M, 4096, D)
        tge = view(M, 5120, 2, 256)
        hse = view(M, 5632, 2, 256)
        oh = view(M, 6144, 2, P)
        ohg = view(M, 6400, 2, P)
        ohT = view(M, 6656, SEQ)
        oh2 = view(M, 6912, 2, P)
        raw_e = [raw[:, 0, :].rearrange("p (a b) -> p a b", a=8), raw[:, 1, :].rearrange("p (a b) -> p a b", a=8),
                 view(M, 8192, 8, 256), view(M, 10240, 8, 256), view(M, 12288, 8, 256), xm[:, :, SEQ:TOK]]
        wse = [view(opr, 4096 * n, 2, 8, 256) for n in range(SPLIT_E)]
        xg = [hx[:, h, 0:2, :].rearrange("p a (b c) -> p (a b) c", c=P) for h in range(2)]
        wflat = wsp[:].rearrange("p a b c -> p (a b c)")
        hT = [wflat[:, h * FE_T * P:(h + 1) * FE_T * P].rearrange("p (a b) -> p a b", b=P) for h in range(2)]

        ident = sb("ident", [P, P])
        rot = sb("rot", [P, P])
        ctab = sb("ctab", [P, 2, SEQ])
        tri, ones, iota = ctab[:, 0, 0:P], ctab[:, 0, P:2 * P], ctab[:, 1, 0:P]
        iota8, iota8b, iotaj = ctab[:, 1, P:P + 8], ctab[:, 1, P + 8:P + 16], ctab[0:1, 1, P + 16:P + 16 + 12]
        wmask = sb("wmask", [P, 2, P])
        cmask = sb("cmask", [P, GRID_W])
        mean = sb("mean", [P, P])
        sel = sb("sel", [4, 2])
        eps = sb("eps", [P, 1])
        vec = sb("vec", [P, 2, V_ALL])
        cc = sb("cc", [P, KT, 2])
        cf = sb("cf", [P, KT, 2])
        c4 = sb("c4", [P, KT, 4], F32R)
        mod = sb("mod", [P, 2, 6, KT, 2])
        am = sb("am", [P, 4, KT, 2])
        bgh = sb("bgh", [P, 24])
        st = sb("st", [P, 4, 5])
        wr = sb("wr", [P, KT, NE])
        br = sb("br", [P, NE])
        rt = view(M, 7168, 1024)
        jobs = sb("jobs", [1, 16], I32)

        pp = [ctx.enter_context(nc.psum_tensor(f"pp{i}", [P, 512], F32)) for i in range(2)]
        S = [ctx.enter_context(nc.psum_tensor(f"S{i}", [P, 512], F32)) for i in range(2)]
        T = [ctx.enter_context(nc.psum_tensor(f"T{i}", [P, 512], F32)) for i in range(2)]
        O = [ctx.enter_context(nc.psum_tensor(f"O{i}", [P, 512], F32)) for i in range(2)]

        raw_full = [sem(f"raw_full{i}") for i in range(2)]
        hi_done, lo_done = sem("hi_done"), sem("lo_done")
        tile_done = sem("tile_done")
        taken = [sem(f"taken{i}") for i in range(2)]
        consts_in, vec_in = sem("consts_in"), sem("vec_in")
        x_in, x_back, rc_in = sem("x_in"), sem("x_back"), sem("rc_in")
        c_ready, eps_ready = sem("c_ready"), sem("eps_ready")
        row_copied, cols_done, mod_ready = sem("row_copied"), sem("cols_done"), sem("mod_ready")
        sq_done, sum_done, sd_done = sem("sq_done"), sem("sum_done"), sem("sd_done")
        scaled, affine, h_split = sem("scaled"), sem("affine"), sem("h_split")
        x_upd = sem("x_upd")
        ob_split, m_split = sem("ob_split"), sem("m_split")
        q2_ready, scores_done, pre_done, exp_done = sem("q2_ready"), sem("scores_done"), sem("pre_done"), sem("exp_done")
        probs_done, pT_done, pT_copied, pv_done = sem("probs_done"), sem("pT_done"), sem("pT_copied"), sem("pv_done")
        o_hi, o_split = sem("o_hi"), sem("o_split")
        bias_in, bias_ready = [sem("bias_in0"), sem("bias_in1")], sem("bias_ready")
        tanh_done, gu_taken, hF_done = sem("tanh_done"), sem("gu_taken"), sem("hF_done")
        act_self, dve_self, pool_self = sem("act_self"), sem("dve_self"), sem("pool_self")
        rt_pe, rt_act, rt_dve, routed, ht_copied = sem("rt_pe"), sem("rt_act"), sem("rt_dve"), sem("routed"), sem("ht_copied")
        yacc_zero = sem("yacc_zero")
        e_raw = [sem(f"e_raw{i}") for i in range(RAW_E)]
        e_hi, e_lo, e_used = sem("e_hi"), sem("e_lo"), sem("e_used")
        e_onehot, e_gath, e_ohT, e_xghi, e_xg = sem("e_onehot"), sem("e_gath"), sem("e_ohT"), sem("e_xghi"), sem("e_xg")
        e_tanh, e_h, e_T, e_hThi, e_hT = sem("e_tanh"), sem("e_h"), sem("e_T"), sem("e_hThi"), sem("e_hT")
        e_yb, e_scat, e_acc = sem("e_yb"), sem("e_scat"), sem("e_acc")
        out_done = sem("out_done")

        g_mix = [0, 0]
        g = 0
        order = []
        nmain = nbr = 0

        def add(array, n, width):
            nonlocal nmain, nbr
            for _ in range(n):
                if array == "main":
                    order.append(("main", nmain, width))
                    nmain += 1
                elif array == "br":
                    order.append(("br", nbr, width))
                    nbr += 1
                else:
                    order.append(array + (width,))

        add("main", ADA_FIRST, 2048)
        g_mix[0] = len(order)
        for s in PLANS[0][0]:
            add(s, 1, 2048 if s == "main" else 1024)
        g_gu, g_dn = [0, 0], [0, 0]
        for h in range(2):
            g_gu[h] = len(order)
            add("main", 2 * F_HALF[h], 2048)
            g_dn[h] = len(order)
            for n in range(DN_STAGE):
                add((f"dn{h}", n), 1, F_HALF[h] * P)
        g_mix[1] = len(order)
        for s in PLANS[1][0]:
            add(s, 1, 2048 if s == "main" else 1024)
        N_SLABS = len(order)
        N_UNITS = 2 * N_SLABS
        width = [w // 2 for _, _, w in order for _ in range(2)]
        last_use = [0] * N_UNITS
        t = 0
        use = [0, 0]
        t_gu, t_dn, use_gu, use_dn = [0, 0], [0, 0], [0, 0], [0, 0]
        mixer_steps = [[], []]
        slot_base = {}

        def plan_mixer(l):
            nonlocal t
            nq = TOK if l == 0 else SEQ
            units = (nq // P) * 8
            rows = []
            _, steps, head, mid, end = PLANS[l]
            flow = [([], s) for s in steps[:head]]
            flow += [([(0, k) for k in sl], s) for sl, s in spread(steps[head:mid], units + 4)]
            flow += [([(1, k) for k in sl], s) for sl, s in spread(steps[mid:end], units + 4)]
            flow += [([], s) for s in steps[end:]]
            bank = 0
            for slots, (what, i, u) in flow:
                gu = None if u is None else 2 * g_mix[l] + u
                t += 1
                use[bank] += 1
                if gu is not None:
                    last_use[gu] = t
                    if what in ("vn", "ada"):
                        last_use[gu + 1] = t
                rows.append(dict(slots=slots, what=what, i=i, u=gu, t=t, bank=bank, use=use[bank], l=l))
                bank = 1 - bank
            assert len(rows) % 2 == 0
            mixer_steps[l] = rows

        for n in range(2 * ADA_FIRST):
            last_use[n] = t = t + 1
        for b in range(2):
            use[b] += ADA_FIRST // 2
        plan_mixer(0)
        for h in range(2):
            t_gu[h], use_gu[h] = t, use[0]
            for n in range(4 * F_HALF[h]):
                last_use[2 * g_gu[h] + n] = t = t + 1
            for b in range(2):
                use[b] += F_HALF[h] // 2
            t_dn[h], use_dn[h] = t, use[0]
            for n in range(2 * DN_STAGE):
                last_use[2 * g_dn[h] + n] = t = t + 1
            for b in range(2):
                use[b] += DN_STAGE // 2
        plan_mixer(1)
        T_DENSE, USE_DENSE = t, list(use)
        def free_to(row):
            end = 2 * (g_mix[row["l"]] + len(PLANS[row["l"]][0])) + 2
            v = row["u"] or 0
            while v < min(end, N_UNITS) and last_use[v - 4] <= row["t"]:
                v += 1
            return v - 1

        step_of = {(l, r["what"], r["i"]): r for l in range(2) for r in mixer_steps[l]}

        def attn_units(l):
            return [(tt, half, qt) for tt in range(4) for half in range(2) for qt in range((TOK if l == 0 else SEQ) // P)]

        unit_base, otile_base, head_base = {}, {}, {}
        ub = ob_ = 0
        for l in range(2):
            for b in range(2):
                unit_base[l, b], otile_base[l, b], head_base[l, b] = ub, ob_, 8 * l
                ub += len(attn_units(l))
                ob_ += 4

        def wait_taken(eng, row):
            eng.wait_ge(taken[row["bank"]], row["use"])

        class Own:
            def __init__(self, eng, s):
                self.eng, self.s, self.base, self.k = eng, s, 0, 0

            def mark(self, ins):
                ins.then_inc(self.s, 1)
                self.k += 1
                return self.base + self.k

            def link(self, ins):
                self.eng.wait_ge(self.s, self.mark(ins))

        def loop(eng, n, body, own=None, first=False):
            k0 = 0
            if first:
                body(0, False)
                k0 = 1
            if own:
                own.base, own.k = own.base + own.k, 0
                start = own.base
            per = [0]
            with eng.Fori(k0, n - 1) as i:
                if own:
                    own.base = start + (i - k0) * body.own_per
                body(i, False)
                if own:
                    per[0] = own.k
                    assert own.k == body.own_per, own.k
            if own:
                own.base, own.k = start + (n - 1 - k0) * per[0], 0
            body(n - 1, True)

        block = ctx.enter_context(nc.Block())

        @block.sync
        def _(sp):
            src = {"main": a["w_main"], "br": a["w_br"], "dn0": a["w_dn0"], "dn1": a["w_dn1"]}
            sp.dma_start(vec[:], a["vec"]).then_inc(vec_in, 16)
            sp.dma_start(cc[:], a["c_both"]).then_inc(vec_in, 16)

            def load(g, slot, arr, idx, w):
                sp.wait_ge(lo_done, 2 * g - 2)
                sp.dma_start(raw[:, slot, 0:w], src[arr][bass.ds(idx, 1), :, :].rearrange("a p n -> (a p) n")
                             ).then_inc(raw_full[slot], 16)

            for g in range(2):
                arr, idx, w = order[g]
                sp.dma_start(raw[:, g, 0:w], src[arr][idx, :, :]).then_inc(raw_full[g], 16)
            sp.dma_start(xm[:], a["x_both"]).then_inc(x_in, 16)
            for g in range(2, ADA_FIRST):
                load(g, g % 2, *order[g])
            sp.dma_start(ident[:], a["ident"]).then_inc(consts_in, 16)
            sp.dma_start(rot[:], a["rot"]).then_inc(consts_in, 16)
            sp.dma_start(ctab[:], a["cossin"]).then_inc(consts_in, 16)
            sp.dma_start(wmask[:], a["wmask"]).then_inc(consts_in, 16)
            sp.dma_start(cmask[:], a["cmask"]).then_inc(consts_in, 16)
            sp.dma_start(wr[:], a["w_router"]).then_inc(consts_in, 16)
            sp.dma_start(br[:], a["b_router"]).then_inc(consts_in, 16)
            g = ADA_FIRST
            while g < N_SLABS:
                n = 1
                pair = order[g:g + 2]
                if len(pair) == 2:
                    step = [(order[g + 2 + k][1] - order[g + k][1]) if g + 2 + k < N_SLABS else 0 for k in range(2)]
                    while g + 2 * n + 1 < N_SLABS and all(
                            order[g + 2 * n + k] == (pair[k][0], pair[k][1] + n * step[k], pair[k][2]) for k in range(2)):
                        n += 1
                if len(pair) == 2 and n > 1:
                    with sp.Fori(0, n) as i:
                        for k in range(2):
                            load(g + k + 2 * i, (g + k) % 2, pair[k][0], pair[k][1] + step[k] * i, pair[k][2])
                    g += 2 * n
                else:
                    load(g, g % 2, *order[g])
                    g += 1
            def expert_slab(e, i, r):
                sp.dma_start(raw_e[i % RAW_E], a["w_moe"][bass.ds(e * JOB_SLABS + r, 1), :, :, :]
                             .rearrange("a p b n -> (a p) b n")).then_inc(e_raw[i % RAW_E], 16)

            sp.wait_ge(m_split, 8 * 2)
            expert_slab(0, RAW_E - 1, RAW_E - 1)
            sp.wait_ge(lo_done, N_UNITS)
            expert_slab(0, 0, 0)
            expert_slab(0, 1, 1)
            sp.wait_ge(affine, 3 * 2 * KT + KT)
            for i in range(2, RAW_E - 1):
                expert_slab(0, i, i)
            sp.wait_ge(routed, 1)
            n_jobs = sp.value_load(jobs[0:1, 12:13], min_val=1, max_val=MAX_JOBS)
            with sp.Fori(1, JOB_SLABS // RAW_E) as r:
                for i in range(RAW_E):
                    sp.wait_ge(e_lo, r * RAW_E + (i + 1))
                    expert_slab(0, i, r * RAW_E + i)
            with sp.Fori(1, n_jobs) as j:
                e = sp.value_load(jobs[0:1, bass.ds(j, 1)], min_val=0, max_val=NE - 1)
                for i in range(JOB_SLABS):
                    sp.wait_ge(e_lo, j * JOB_SLABS + (i + 1))
                    expert_slab(e, i, i)
            e = sp.value_load(jobs[0:1, bass.ds(n_jobs, 1)], min_val=0, max_val=NE - 1)
            for i in range(2):
                sp.wait_ge(e_lo, n_jobs * JOB_SLABS + (i + 1))
                expert_slab(e, i, i)
            sp.wait_ge(x_upd, 8 * 4)
            sp.dma_start(out, xm[:, :, 0:SEQ]).then_inc(out_done, 16)
            sp.wait_ge(out_done, 16)

        @block.gpsimd
        def _(pool):
            own = Own(pool, pool_self)
            pool.memset(eps[:], EPS).then_inc(eps_ready, 1)
            pool.memset(mean[:], 1.0 / D).then_inc(eps_ready, 1)
            own.link(pool.memset(sel[:], 0.0))
            own.link(pool.affine_select(out=sel[:], in_=sel[:], compare_op=ALU.not_equal, fill=1.0,
                                        base=0, pattern=[[-1, 2]], channel_multiplier=1))
            pool.affine_select(out=sel[:], in_=sel[:], compare_op=ALU.not_equal, fill=1.0,
                               base=-2, pattern=[[-1, 2]], channel_multiplier=1).then_inc(eps_ready, 1)

            own.link(pool.memset(q2, 0.0))

            def mask_bias(l, head):
                pool.wait_ge(bias_in[head % 2], 16 * (4 * l + head // 2 + 1))
                bv = bias[:, head % 2, :, :].rearrange("p a (b c) -> p (a b) c", c=GRID_W)
                cm = cmask[:].rearrange("p (a c) -> p a c", a=1).to_broadcast([P, 8, GRID_W])
                pool.tensor_tensor(bv, bv, cm, ALU.add).then_inc(bias_ready, 1)
                pool.wait_ge(bias_ready, head_base[l, 1] + head + 1)

            for l in range(2):
                nq = TOK if l == 0 else SEQ
                for row in mixer_steps[l]:
                    for b, s in row["slots"]:
                        units = attn_units(l)
                        if s >= len(units):
                            continue
                        tt, half, qt = units[s]
                        w = unit_base[l, b] + s
                        if b == 1 and s == 0:
                            mask_bias(l, 0)
                        wait_taken(pool, step_of[l, "rope_q" if b == 0 else "qn", tt])
                        if w >= 2:
                            pool.wait_ge(scores_done, w - 1)
                        src = (qa if b == 0 else qn)[64 * half:64 * half + 64, tt, P * qt:P * qt + P]
                        pool.tensor_copy(q2[64 * half:64 * half + 64, half, w % 2, :], src).then_inc(q2_ready, 1)
                        pool.wait_ge(q2_ready, w + 1)
                        if b == 1 and qt == nq // P - 1 and s + 1 < len(units):
                            mask_bias(l, 2 * tt + half + 1)
            pool.wait_ge(routed, 1)
            pool.memset(yacc, 0.0).then_inc(yacc_zero, 1)
            pool.wait_ge(yacc_zero, 1)

        @block.scalar
        def _(act):
            own = Own(act, act_self)
            nxt = [0]

            def split_hi(u, slot, half, w, gval, tdep):
                if half == 0:
                    act.wait_ge(raw_full[slot // 2], gval)
                if tdep is not None:
                    act.wait_ge(tile_done, tdep)
                act.activation(wsp[:, slot, 0, 0:w], raw[:, slot // 2, half * w:half * w + w], ACT.Copy
                               ).then_inc(hi_done, 1)

            def split_to(u):
                while nxt[0] <= u and nxt[0] < N_UNITS:
                    n = nxt[0]
                    split_hi(n, n % 4, n % 2, width[n], 16 * (n // 4 + 1), last_use[n - 4] if n >= 4 else None)
                    nxt[0] += 1

            def stage_ahead(u0, t0, w, i, s, last, n=2):
                if last and s == n - 1:
                    split_to(nxt[0] + 1)
                    return
                for h in range(2):
                    ur = 2 * (s + 1) + h
                    td = t0 + 2 * n * i + ur - 3
                    if isinstance(td, int) and td < 1:
                        td = None
                    split_hi(None, (u0 + ur) % 4, h, w, 16 * ((u0 + ur) // 4 + 1) + 8 * n * i, td)
                if last:
                    nxt[0] += 2

            act.wait_ge(vec_in, 32)
            act.activation(cf[:], cc[:], ACT.Tanh, scale=0.5).then_inc(c_ready, 1)

            def norm_root(n, N):
                act.wait_ge(sum_done, 8 * (n + 1))
                act.activation(sd[:, 0:N], O[1][:, 0:N], ACT.Sqrt, bias=eps[:]).then_inc(sd_done, 1)

            def square(src, n, k, N):
                if 8 * n + k >= 2:
                    act.wait_ge(sum_done, 8 * n + k - 1)
                act.activation(sq[:, k % 2, 0:N], src, ACT.Square).then_inc(sq_done, 1)

            def ada():
                split_to(1)
                for s in range(ADA_FIRST):
                    split_to(2 * s + 3)
                    act.wait_ge(tile_done, 2 * s + 2)
                    act.activation(adr_f[:, s % 2, :], pp[s % 2][0:4, 0:256], ACT.Copy).then_inc(taken[s % 2], 1)
                    for k in FIRST_NORM[s]:
                        if k == 0:
                            act.wait_ge(x_in, 16)
                        square(xm[:, k, :], 0, k, TOK)

            def prenorm(n, l, which, N, hcount):
                if n == 0:
                    act.wait_ge(eps_ready, 3)
                else:
                    for k in range(KT):
                        act.wait_ge(x_upd, 8 * hcount[0] + k + 1)
                        square(xm[:, k, 0:N], n, k, N)
                norm_root(n, N)
                act.wait_ge(mod_ready, (1, 2, 3, 3)[n // 2])
                for k in range(KT):
                    act.wait_ge(scaled, 8 * (n // 2) + k + 1)
                    for s in range(N // SEQ):
                        c = slice(SEQ * s, SEQ * s + SEQ)
                        dst = hfa[:, k, :] if n == 6 else hx[:, 0, k, c]
                        act.activation(dst, gt[:, k % 2, c], ACT.Identity, bias=mod[:, l, 3 * which, k, s:s + 1]
                                       ).then_inc(affine, 1)

            def load_bias(l, head):
                act.dma_start(bias[:, head % 2, :, :], a["rpb_rows"][l, head]).then_inc(bias_in[head % 2], 16)

            def attn(l, b, s):
                units = attn_units(l)
                nqt = (TOK if l == 0 else SEQ) // P
                if 0 <= s - 2 < len(units):
                    w = unit_base[l, b] + s - 2
                    kts = 4 if units[s - 2][2] < 2 else 2
                    act.wait_ge(pT_done, w + 1)
                    if w >= 2:
                        act.wait_ge(pv_done, w - 1)
                    act.activation(prT[:, w % 2, 0:kts, :], T[w % 2][:, 0:kts * P].rearrange("p (a b) -> p a b", b=P),
                                   ACT.Copy).then_inc(pT_copied, 1)
                if s < len(units):
                    tt, half, qt = units[s]
                    w = unit_base[l, b] + s
                    n = TOK if qt < 2 else SEQ
                    sc = st[:, w % 4, :]
                    act.wait_ge(pre_done, w + 1)
                    if b == 1 and qt == 0 and 1 <= 2 * tt + half < 7:
                        load_bias(l, 2 * tt + half + 1)
                    if b == 0:
                        head = tt + 4 * half
                        own.link(act.activation(sc[:, 3:4], vec[:, l, V_SINK + head:V_SINK + head + 1], ACT.Exp, bias=sc[:, 1:2]))
                    if w >= 2:
                        act.wait_ge(pT_done, w - 1)
                    act.activation(pr[:, w % 2, 0:n], S[w % 2][:, 0:n], ACT.Exp, bias=sc[:, 1:2],
                                   accum_out=sc[:, 2:3]).then_inc(exp_done, 1)
                if 0 <= s - 4 < len(units) and (s - 4) % (2 * nqt) == 2 * nqt - 1:
                    tt = units[s - 4][0]
                    ot = otile_base[l, b] + tt
                    act.wait_ge(pv_done, unit_base[l, b] + s - 3)
                    act.activation(o_br[2 * b][:, 0, tt, 0:nqt * P], O[ot % 2][:, 0:nqt * P], ACT.Copy).then_inc(o_hi, 1)

            def mixer(l, nn, hcount):
                nq = TOK if l == 0 else SEQ
                for row in mixer_steps[l]:
                    for b, s in row["slots"]:
                        attn(l, b, s)
                    what, i, u, bank = row["what"], row["i"], row["u"], row["bank"]
                    if u is not None:
                        split_to(u + 2 + (what in ("vn", "ada")))
                    src = pp[bank]

                    def take(dst, s=None, scale=1.0, func=ACT.Copy, **kw):
                        act.wait_ge(tile_done, row["t"])
                        act.activation(dst, s if s is not None else src[:, 0:nq], func, scale=scale, **kw
                                       ).then_inc(taken[bank], 1)
                    if what == "ada":
                        n = ADA_MIXER.index(i)
                        if n >= 2:
                            act.wait_ge(tile_done, step_of[l, "ada_t", ADA_MIXER[n - 2]]["t"])
                        take(ada_rows(n), src[0:4, 0:256])
                    elif what == "ka":
                        take(ka, src[:, :])
                    elif what == "va":
                        take(vat, src[:, :])
                    elif what == "va_t":
                        take(V[:, :, 0:P], src[:, :].rearrange("p (a b) -> p a b", b=P))
                    elif what == "qa":
                        take(qa[:, i, 0:nq], scale=HD ** -0.5)
                    elif what == "qn":
                        if i == 0:
                            act.wait_ge(ob_split, 4 * (l + 1))
                        take(qn[:, i, 0:nq], scale=HD ** -0.5)
                    elif what == "kn":
                        take(kn[:, i, :], src[:, :])
                    elif what == "vn":
                        s, tp = i
                        if i == (1, 0):
                            act.wait_ge(h_split, 8 * (2 * l + 1))
                            if l == 0:
                                wait_taken(act, step_of[0, "ada_t", ADA_MIXER[ADA_BESIDE_A - 1]])
                            load_bias(l, 0)
                            load_bias(l, 1)
                        take(V[:, 2 * tp:2 * tp + 2, P + 256 * s:P + 256 * s + 256],
                             src[:, :].rearrange("p (a b) -> p a b", b=256))
                    elif what == "ux":
                        if i >= 2:
                            wait_taken(act, step_of[l, "gc", i - 2])
                        take(gt[:, i % 2, 0:nq])
                    elif what == "gx":
                        r, n = i
                        if n >= 2 or r:
                            wait_taken(act, step_of[l, "br", (r, n - 2) if n >= 2 else (r - 1, n + 6)])
                        take(gt[:, n % 2, 0:nq], func=ACT.Tanh, scale=0.5, bias=bgh[:, 8 * r + n:8 * r + n + 1])
                    elif what == "wout":
                        act.wait_ge(tile_done, row["t"])
                        if i == 0 and l == 0:
                            act.wait_ge(m_split, 8)
                            act.dma_start(xm[:], a["x_both"]).then_inc(x_back, 16)
                        square(src[:, 0:nq], nn, i, nq)
                        act.activation(y[:, i, 0:nq], src[:, 0:nq], ACT.Copy).then_inc(taken[bank], 1)
                    if what in ("ada", "br") or (l == 1 and what == "gx"):
                        split_to(free_to(row))
                norm_root(nn, nq)

            def ffn():
                for h in range(2):
                    u0, t0, nF = 2 * g_gu[h], t_gu[h], F_HALF[h]
                    split_to(u0 + 1)
                    n = nF // 2
                    nxt[0] = u0 + 8 * (n - 1) + 2

                    def body(i, last):
                        for s in range(2):
                            stage_ahead(u0, t0, 1024, i, 2 * s, last, 4)
                            act.wait_ge(tile_done, t0 + 8 * i + 4 * s + 1)
                            act.activation(gt[:, s, :], S[s][:, :], ACT.Tanh, scale=0.5).then_inc(tanh_done, 1)
                            stage_ahead(u0, t0, 1024, i, 2 * s + 1, last, 4)
                            act.wait_ge(tile_done, t0 + 8 * i + 4 * s + 4)
                            act.activation(adr_f[:, s, :], pp[s][0:4, 0:256], ACT.Copy).then_inc(taken[s], 1)
                    body.own_per = 0
                    loop(act, n, body)
                    u0, t0 = 2 * g_dn[h], t_dn[h]
                    w = nF * P // 2
                    if h == 0:
                        split_to(u0 + 1)
                        n = DN_STAGE // 2
                        nxt[0] = u0 + 4 * (n - 1) + 2

                        def body(i, last):
                            for s in range(2):
                                stage_ahead(u0, t0, w, i, s, last)
                                act.wait_ge(tile_done, t0 + 4 * i + 2 * s + 2)
                                act.activation(y[:, bass.ds(2 * i + s, 1), :], pp[s][:, :].rearrange("p (a b) -> p a b", a=1),
                                               ACT.Copy).then_inc(taken[s], 1)
                        body.own_per = 0
                        loop(act, n, body)
                    else:
                        for n in range(KT):
                            split_to(u0 + 2 * n + 3)
                            act.wait_ge(taken[n % 2], use_dn[1] + n // 2 + 1)
                            square(y[:, n, :], 3, n, TOK)
                norm_root(3, TOK)

            ada()
            prenorm(0, 0, 0, TOK, (0, 0))
            mixer(0, 1, None)
            prenorm(2, 0, 1, TOK, (0, 1))
            ffn()
            prenorm(4, 1, 0, TOK, (1, 2))
            mixer(1, 5, None)
            wait_taken(act, step_of[1, "rope_q", 3])
            act.dma_start(ctab[:], a["routing"]).then_inc(rc_in, 16)
            prenorm(6, 1, 1, SEQ, (2, 3))

            for n in range(4):
                act.wait_ge(rt_pe, n + 1)
                act.activation(ht[:, n // 2, 512 * (n % 2):512 * (n % 2) + 512], [pp[0], pp[1], S[0], S[1]][n][:, :],
                               ACT.Copy).then_inc(ht_copied, 1)
            act.wait_ge(rt_dve, 1)
            act.activation(rt[:, 8:10], rt[:, 10:12], ACT.Exp).then_inc(rt_act, 1)
            act.wait_ge(routed, 1)
            n_jobs = act.value_load(jobs[0:1, 12:13], min_val=1, max_val=MAX_JOBS)

            def hi(j, i):
                act.wait_ge(e_raw[i % RAW_E], j * (16 * JOB_SLABS // RAW_E) + 16 * (i // RAW_E + 1))
                act.wait_ge(e_used, j * JOB_SLABS + (i + 1))
                act.activation(wse[i % SPLIT_E][:, 0, :, :], raw_e[i % RAW_E], ACT.Copy).then_inc(e_hi, 1)

            def xg_hi(j):
                act.wait_ge(e_gath, 2 * j + 1)
                for n in range(2):
                    act.activation(xg[0][:, 4 * n:4 * n + 4, :], pp[n][:, :].rearrange("p (a b) -> p a b", b=P),
                                   ACT.Copy).then_inc(e_xghi, 1)

            hi(0, 0)
            xg_hi(0)
            hi(0, 1)
            with act.Fori(0, n_jobs) as j:
                def hT_hi(q):
                    act.wait_ge(e_T, j * GU_GROUPS + (q + 1))
                    act.activation(hT[0][:, 2 * q:2 * q + 2, :], T[q % 2][:, 0:256].rearrange("p (a b) -> p a b", b=P),
                                   ACT.Copy).then_inc(e_hThi, 1)

                for q in range(GU_GROUPS):
                    hi(j, 2 * q + 2)
                    hi(j, 2 * q + 3)
                    act.wait_ge(e_used, j * JOB_SLABS + (2 * q + 2 + SPLIT_E))
                    act.activation(tge[:, q % 2, :], S[q % 2][:, 0:256], ACT.Tanh, scale=0.5).then_inc(e_tanh, 1)
                    if q == 1:
                        act.wait_ge(e_gath, 2 * j + 2)
                        act.activation(ohT, T[1][:, 0:SEQ], ACT.Copy).then_inc(e_ohT, 1)
                    if q:
                        hT_hi(q - 1)
                for d in range(DN_SLABS):
                    hi(j, GU_SLABS + d + 2)
                    if d == 0:
                        hT_hi(GU_GROUPS - 1)
                act.wait_ge(e_used, j * JOB_SLABS + (JOB_SLABS + SPLIT_E))
                for n in range(2):
                    act.activation(yb[:, 512 * n:512 * n + 512], O[n][:, :], ACT.Copy).then_inc(e_yb, 1)
                xg_hi(j + 1)
            act.wait_ge(e_acc, n_jobs * 4 + 4)
            for k in range(KT):
                square(yacc[:, k, :], 7, k, SEQ)
            norm_root(7, SEQ)

        @block.vector
        def _(dve):
            own = Own(dve, dve_self)
            nxt = [0]

            def split_lo(hval, slot, half, w):
                dve.wait_ge(hi_done, hval)
                dve.tensor_tensor(wsp[:, slot, 1, 0:w], raw[:, slot // 2, half * w:half * w + w],
                                  wsp[:, slot, 0, 0:w], ALU.subtract).then_inc(lo_done, 1)

            def split_to(u):
                while nxt[0] <= u and nxt[0] < N_UNITS:
                    n = nxt[0]
                    split_lo(n + 1, n % 4, n % 2, width[n])
                    nxt[0] += 1

            def stage_ahead(u0, w, i, s, last, n=2):
                if last and s == n - 1:
                    split_to(nxt[0] + 1)
                    return
                for h in range(2):
                    ur = 2 * (s + 1) + h
                    split_lo(u0 + ur + 1 + 2 * n * i, (u0 + ur) % 4, h, w)
                if last:
                    nxt[0] += 2

            dve.memset(rt[0:1, 0:1], 0.0).then_inc(gu_taken, 2)
            dve.wait_ge(c_ready, 1)
            own.link(dve.scalar_tensor_tensor(cf[:], cf[:], 1.0, cc[:], ALU.add, ALU.mult))
            own.link(dve.tensor_scalar(c4[:, :, 0:2], cf[:], 0.5, None, ALU.mult))
            dve.scalar_tensor_tensor(c4[:, :, 2:4], cf[:], 0.5, c4[:, :, 0:2], ALU.mult, ALU.subtract).then_inc(c_ready, 1)

            def mod_add(l, first, src):
                n = src.shape[1] // 2
                b = vec[:, l, V_BADA + 2 * first:V_BADA + 2 * first + n].rearrange("p (a c) -> p a c", c=1).to_broadcast([P, n, 2])
                dst = mod[:, l].rearrange("p a b c -> p (a b) c")[:, 2 * first:2 * first + n, :]
                return dve.tensor_tensor(dst, src.rearrange("p (a c) -> p a c", c=2), b, ALU.add)

            def am_part(l, part):
                v = (V_GPRE, V_GPOST, V_GPREF, V_GPOSTF)[part]
                gv = vec[:, l, v:v + 8].rearrange("p (a c) -> p a c", c=1).to_broadcast([P, 8, 2])
                if part % 2 == 0:
                    return dve.scalar_tensor_tensor(am[:, part], mod[:, l, 3 * (part // 2) + 1], 1.0, gv, ALU.add, ALU.mult)
                return dve.tensor_tensor(am[:, part], mod[:, l, 3 * (part // 2) + 2], gv, ALU.mult)

            def gate_bias(l):
                dve.tensor_scalar(bgh[:], vec[:, l, V_BGATE:V_BGATE + 24], 0.5, None, ALU.mult).then_inc(mod_ready, 1)

            def ada():
                split_to(1)
                n = ADA_FIRST // 2
                nxt[0] = 4 * (n - 1) + 2

                def body(i, last):
                    for s in range(2):
                        stage_ahead(0, 1024, i, s, last)
                body.own_per = 0
                loop(dve, n, body)
                dve.wait_ge(cols_done, ADA_FIRST)
                own.link(mod_add(0, 0, T[0][:, 0:4 * ADA_FIRST]))
                own.link(am_part(0, 0))
                gate_bias(0)

            def prenorm(n, l, which, N):
                dve.wait_ge(sd_done, n + 1)
                own.link(dve.reciprocal(rs[:, 0:N], sd[:, 0:N]))
                ns = N // SEQ
                for k in range(KT + 1):
                    if k < KT:
                        if k >= 2:
                            dve.wait_ge(affine, aff[0] + (k - 1) * ns)
                            if n < 6:
                                dve.wait_ge(h_split, 8 * (n // 2) + k - 1)
                        for s in range(ns):
                            c = slice(SEQ * s, SEQ * s + SEQ)
                            ins = dve.scalar_tensor_tensor(gt[:, k % 2, c], xm[:, k, c], am[:, 2 * which, k, s:s + 1],
                                                           rs[:, c], ALU.mult, ALU.mult)
                            if s == ns - 1:
                                ins.then_inc(scaled, 1)
                            else:
                                own.mark(ins)
                    if k >= 1 and n < 6:
                        dve.wait_ge(affine, aff[0] + k * ns)
                        for s in range(ns):
                            c = slice(SEQ * s, SEQ * s + SEQ)
                            ins = dve.scalar_tensor_tensor(hx[:, 1, k - 1, c], gt[:, (k - 1) % 2, c], mod[:, l, 3 * which, k - 1, s:s + 1],
                                                           hx[:, 0, k - 1, c], ALU.add, ALU.subtract)
                            if s == ns - 1:
                                ins.then_inc(h_split, 1)
                            else:
                                own.mark(ins)
                aff[0] += KT * ns

            aff = [0]

            def postnorm(n, l, which, N, src):
                dve.wait_ge(sd_done, n + 1)
                own.link(dve.reciprocal(rs[:, 0:N], sd[:, 0:N]))
                if n == 1:
                    dve.wait_ge(x_back, 16)
                at = {}
                for k in range(KT + 1):
                    if k < KT:
                        if k >= 3:
                            dve.wait_ge(x_upd, 8 * pm[0] + k - 2)
                        at[k] = own.mark(dve.tensor_tensor(gt3[:, k % 3, 0:N], src[:, k, 0:N], rs[:, 0:N], ALU.mult))
                    if k:
                        dve.wait_ge(dve_self, at[k - 1])
                        for s in range(N // SEQ):
                            c = slice(SEQ * s, SEQ * s + SEQ)
                            ins = dve.scalar_tensor_tensor(xm[:, k - 1, c], gt3[:, (k - 1) % 3, c], am[:, 2 * which + 1, k - 1, s:s + 1],
                                                           xm[:, k - 1, c], ALU.mult, ALU.add)
                            if s == N // SEQ - 1:
                                ins.then_inc(x_upd, 1)
                            else:
                                own.mark(ins)
                pm[0] += 1

            pm = [0]

            def attn(l, b, s):
                units = attn_units(l)
                nqt = (TOK if l == 0 else SEQ) // P
                if s < len(units):
                    tt, half, qt = units[s]
                    w = unit_base[l, b] + s
                    n = TOK if qt < 2 else SEQ
                    sc = st[:, w % 4, :]
                    bank = S[w % 2]
                    dve.wait_ge(scores_done, w + 1)
                    if qt < 2:
                        if b == 0:
                            c = slice(P, 2 * P) if qt == 0 else slice(0, P)
                            own.link(dve.tensor_tensor(bank[:, c], bank[:, c], wmask[:, qt, :], ALU.add))
                        else:
                            dve.wait_ge(bias_ready, head_base[l, b] + 2 * tt + half + 1)
                            own.link(dve.tensor_tensor(bank[:, 0:SEQ], bank[:, 0:SEQ], bias[:, half, qt, :], ALU.add))
                    own.link(dve.reduce_max(sc[:, 0:1], bank[:, 0:n], AX.X))
                    if b == 0:
                        head = tt + 4 * half
                        dve.tensor_scalar(sc[:, 1:2], sc[:, 0:1], vec[:, l, V_SINK + head:V_SINK + head + 1], -1.0,
                                          ALU.max, ALU.mult).then_inc(pre_done, 1)
                    else:
                        dve.tensor_scalar(sc[:, 1:2], sc[:, 0:1], -1.0, None, ALU.mult).then_inc(pre_done, 1)
                if 0 <= s - 1 < len(units):
                    w = unit_base[l, b] + s - 1
                    n = TOK if units[s - 1][2] < 2 else SEQ
                    sc = st[:, w % 4, :]
                    dve.wait_ge(exp_done, w + 1)
                    if b == 0:
                        own.link(dve.tensor_tensor(sc[:, 2:3], sc[:, 2:3], sc[:, 3:4], ALU.add))
                    own.link(dve.reciprocal(sc[:, 4:5], sc[:, 2:3]))
                    dve.tensor_scalar(pr[:, w % 2, 0:n], pr[:, w % 2, 0:n], sc[:, 4:5], None, ALU.mult).then_inc(probs_done, 1)
                if 0 <= s - 4 < len(units) and (s - 4) % (2 * nqt) == 2 * nqt - 1:
                    tt = units[s - 4][0]
                    ot = otile_base[l, b] + tt
                    dve.wait_ge(o_hi, ot + 1)
                    dve.tensor_tensor(o_br[2 * b][:, 1, tt, 0:nqt * P], O[ot % 2][:, 0:nqt * P],
                                      o_br[2 * b][:, 0, tt, 0:nqt * P], ALU.subtract).then_inc(o_split, 1)

            tmp_read = [None]

            def mixer(l):
                nq = TOK if l == 0 else SEQ
                mg = xm if l == 0 else xm[:, :, SEQ:TOK]
                for row in mixer_steps[l]:
                    for b, s in row["slots"]:
                        attn(l, b, s)
                    what, i, u, bank = row["what"], row["i"], row["u"], row["bank"]
                    if u is not None:
                        split_to(u + 2 + (what in ("vn", "ada")))
                    src = pp[bank]
                    if what in ("rope_q", "rope_k"):
                        v = qa[:, i, 0:SEQ] if what == "rope_q" else ka[:, 0:SEQ]
                        dve.wait_ge(tile_done, row["t"])
                        if tmp_read[0] is not None:
                            wait_taken(dve, tmp_read[0])
                        tmp_read[0] = row
                        own.link(dve.tensor_tensor(tmp[:, 0:SEQ], src[:, 0:SEQ], ctab[:, 1, :], ALU.mult))
                        own.link(dve.tensor_tensor(v, v, ctab[:, 0, :], ALU.mult))
                        dve.tensor_tensor(v, v, tmp[:, 0:SEQ], ALU.add).then_inc(taken[bank], 1)
                    elif what == "ada_t":
                        dve.wait_ge(tile_done, row["t"])
                        mod_add(i[0], i[1], src[:, 0:4]).then_inc(taken[bank], 1)
                    elif what == "gc":
                        dve.wait_ge(tile_done, row["t"])
                        wait_taken(dve, step_of[l, "ux", i])
                        u = cu[:, i % 2, :]
                        dve.tensor_tensor(u[:, 0:nq], src[:, 0:nq], gt[:, i % 2, 0:nq], ALU.mult).then_inc(taken[bank], 1)
                        wait_taken(dve, row)
                        wv = lambda k: vec[:, l, V_CONV + 4 * k + i:V_CONV + 4 * k + i + 1]
                        own.link(dve.tensor_scalar(cv[:, i, 0:nq], u[:, 0:nq], wv(1), None, ALU.mult))
                        for s0 in range(0, nq, SEQ):
                            for k, to, fr in ((0, 1, 0), (2, 0, 1)):
                                v = cv[:, i, s0 + to:s0 + SEQ - fr]
                                own.link(dve.scalar_tensor_tensor(v, u[:, s0 + fr:s0 + SEQ - to], wv(k), v, ALU.mult, ALU.add))
                    elif what == "gb":
                        dve.wait_ge(tile_done, row["t"])
                        if i >= 2:
                            dve.wait_ge(ob_split, 4 * l + i - 1)
                        dve.tensor_tensor(ob[:, i % 2, 0:nq], src[:, 0:nq], cv[:, i, 0:nq], ALU.mult).then_inc(taken[bank], 1)
                        wait_taken(dve, row)
                        own.link(dve.tensor_copy(o_br[1][:, 0, i, 0:nq], ob[:, i % 2, 0:nq]))
                        dve.tensor_tensor(o_br[1][:, 1, i, 0:nq], ob[:, i % 2, 0:nq], o_br[1][:, 0, i, 0:nq],
                                          ALU.subtract).then_inc(ob_split, 1)
                    elif what == "br":
                        r, n = i
                        dve.wait_ge(tile_done, row["t"])
                        wait_taken(dve, step_of[l, "gx", i])
                        dst = mg[:, n, 0:nq] if r == 0 else tmp[:, 0:nq]
                        if tmp_read[0] is not None:
                            wait_taken(dve, tmp_read[0])
                            tmp_read[0] = None
                        dve.scalar_tensor_tensor(dst, gt[:, n % 2, 0:nq], 1.0, src[:, 0:nq], ALU.add, ALU.mult
                                                 ).then_inc(taken[bank], 1)
                        wait_taken(dve, row)
                        if r:
                            own.link(dve.tensor_tensor(mg[:, n, 0:nq], mg[:, n, 0:nq], tmp[:, 0:nq], ALU.add))
                        if r == 2:
                            own.link(dve.tensor_scalar(m_sp[:, 0, n, 0:nq], mg[:, n, 0:nq], 0.5, None, ALU.mult))
                            dve.scalar_tensor_tensor(m_sp[:, 1, n, 0:nq], mg[:, n, 0:nq], 0.5, m_sp[:, 0, n, 0:nq],
                                                     ALU.mult, ALU.subtract).then_inc(m_split, 1)
                    if what in ("ada", "br") or (l == 1 and what == "gx"):
                        split_to(free_to(row))

            def ffn():
                for h in range(2):
                    u0, t0, nF = 2 * g_gu[h], t_gu[h], F_HALF[h]
                    split_to(u0 + 1)
                    n = nF // 2
                    nxt[0] = u0 + 8 * (n - 1) + 2
                    f0 = h * F_HALF[0]

                    def body(i, last):
                        for s in range(2):
                            stage_ahead(u0, 1024, i, 2 * s, last, 4)
                            stage_ahead(u0, 1024, i, 2 * s + 1, last, 4)
                            dve.wait_ge(tile_done, t0 + 8 * i + 4 * s + 2)
                            dve.wait_ge(tanh_done, f0 + 2 * i + s + 1)
                            own.link(dve.scalar_tensor_tensor(gt[:, s, :], gt[:, s, :], 1.0, S[s][:, :], ALU.add, ALU.mult))
                            dve.scalar_tensor_tensor(hf2[:, s, :], gt[:, s, :], 0.5, T[s][:, :], ALU.mult, ALU.mult
                                                     ).then_inc(gu_taken, 1)
                            dve.wait_ge(gu_taken, f0 + 2 * i + s + 3)
                            f = bass.ds(2 * i + s, 1)
                            hv = hf2[:, s, :].rearrange("p (a b) -> p a b", a=1)
                            own.link(dve.tensor_copy(hF[:, 0, f, :], hv))
                            dve.tensor_tensor(hF[:, 1, f, :], hv, hF[:, 0, f, :], ALU.subtract).then_inc(hF_done, 1)
                            dve.wait_ge(hF_done, f0 + 2 * i + s + 1)
                    body.own_per = 4
                    loop(dve, n, body, own)
                    u0 = 2 * g_dn[h]
                    w = nF * P // 2
                    if h == 0:
                        split_to(u0 + 1)
                        n = DN_STAGE // 2
                        nxt[0] = u0 + 4 * (n - 1) + 2

                        def body(i, last):
                            for s in range(2):
                                stage_ahead(u0, w, i, s, last)
                        body.own_per = 0
                        loop(dve, n, body)
                    else:
                        for n in range(KT):
                            split_to(u0 + 2 * n + 3)
                            dve.wait_ge(tile_done, t_dn[1] + 2 * n + 2)
                            dve.tensor_tensor(y[:, n, :], pp[n % 2][:, :], y[:, n, :], ALU.add).then_inc(taken[n % 2], 1)

            ada()
            prenorm(0, 0, 0, TOK)
            mixer(0)
            for part in (1, 2):
                own.link(am_part(0, part))
            am_part(0, 3).then_inc(mod_ready, 1)
            postnorm(1, 0, 0, TOK, y)
            prenorm(2, 0, 1, TOK)
            ffn()
            postnorm(3, 0, 1, TOK, y)
            dve.wait_ge(cols_done, ADA_FIRST + ADA_FFN)
            own.link(mod_add(1, ADA_SLABS - ADA_FFN, O[0][:, 0:4 * ADA_FFN]))
            for part in range(4):
                own.link(am_part(1, part))
            gate_bias(1)
            prenorm(4, 1, 0, TOK)
            mixer(1)
            postnorm(5, 1, 0, SEQ, y)
            prenorm(6, 1, 1, SEQ)

            L = rt[:, 16:32].rearrange("p (a b) -> p a b", b=NE)
            O1 = rt[:, 32:48].rearrange("p (a b) -> p a b", b=NE)
            O2 = rt[:, 48:64].rearrange("p (a b) -> p a b", b=NE)
            X1 = rt[:, 64:80].rearrange("p (a b) -> p a b", b=NE)
            AS = rt[:, 80:96].rearrange("p (a b) -> p a b", b=NE)
            mx = rt[:, 12:16]
            ix = rt[:, 96:98]
            cn, nb, ea, eb = rt[:, 104:112], rt[:, 112:120], rt[:, 120:128], rt[:, 128:136]

            def b8(v):
                return v.rearrange("p (a c) -> p a c", c=1).to_broadcast([P, 2, NE])

            def c8(v):
                return v.rearrange("p (a c) -> p a c", a=1).to_broadcast([P, 2, NE])

            dve.wait_ge(rt_pe, 5)
            dve.wait_ge(rc_in, 16)
            own.link(dve.tensor_tensor(L, O[0][:, 0:16].rearrange("p (a b) -> p a b", b=NE), c8(br[:]), ALU.add))
            for n, o in enumerate((O1, O2)):
                own.link(dve.tensor_reduce(mx[:, 2 * n:2 * n + 2], L, AX.X, ALU.max))
                own.link(dve.tensor_tensor(X1, L, b8(mx[:, 2 * n:2 * n + 2]), ALU.is_equal))
                own.link(dve.scalar_tensor_tensor(X1, X1, -99.0, c8(iota8b), ALU.mult, ALU.add))
                own.link(dve.tensor_reduce(ix, X1, AX.X, ALU.min))
                own.link(dve.tensor_tensor(o, c8(iota8), b8(ix), ALU.is_equal))
                if n == 0:
                    own.link(dve.scalar_tensor_tensor(L, o, -BIG, L, ALU.mult, ALU.add))
            dve.tensor_tensor(rt[:, 10:12], mx[:, 2:4], mx[:, 0:2], ALU.subtract).then_inc(rt_dve, 1)
            dve.tensor_tensor(AS, O1, O2, ALU.add).then_inc(rt_dve, 1)
            dve.wait_ge(rt_act, 1)
            own.link(dve.tensor_scalar(rt[:, 98:100], rt[:, 8:10], 1.0, None, ALU.add))
            own.link(dve.reciprocal(rt[:, 4:6], rt[:, 98:100]))
            own.link(dve.tensor_tensor(rt[:, 6:8], rt[:, 4:6], rt[:, 8:10], ALU.mult))
            dve.wait_ge(rt_pe, 6)
            own.link(dve.tensor_copy(cn, O[0][:, 48:56]))
            own.link(dve.tensor_scalar(nb, cn, 0.5, None, ALU.is_ge))
            own.link(dve.memset(nb[:, 0:1], 1.0))
            own.link(dve.tensor_scalar(ea, cn, P + 0.5, None, ALU.is_ge))
            own.link(dve.tensor_tensor(nb, nb, ea, ALU.add))
            src, dst = nb, ea
            for sh in (1, 2, 4):
                own.link(dve.tensor_copy(dst[:, 0:sh], src[:, 0:sh]))
                own.link(dve.tensor_tensor(dst[:, sh:8], src[:, sh:8], src[:, 0:8 - sh], ALU.add))
                src, dst = dst, (eb if dst is ea else ea)
            end, beg = src, rt[:, 136:144]
            own.link(dve.tensor_tensor(beg, end, nb, ALU.subtract))
            own.link(dve.scalar_tensor_tensor(AS, c8(beg), float(P), O[0][:, 32:48].rearrange("p (a b) -> p a b", b=NE),
                                              ALU.mult, ALU.add))
            for n, o in enumerate((O1, O2)):
                own.link(dve.tensor_tensor(X1, AS, o, ALU.mult))
                own.link(dve.reduce_sum(rt[:, 2 * n:2 * n + 2], X1, AX.X))
            cmp = rt[0:1, 256:256 + 96].rearrange("p (a b) -> p a b", b=NE)
            own.link(dve.tensor_tensor(cmp, iotaj.rearrange("p (a c) -> p a c", c=1).to_broadcast([1, 12, NE]),
                                       end[0:1, :].rearrange("p (a c) -> p a c", a=1).to_broadcast([1, 12, NE]), ALU.is_ge))
            own.link(dve.reduce_sum(rt[0:1, 144:156], cmp, AX.X))
            own.link(dve.tensor_scalar(jobs[0:1, 0:12], rt[0:1, 144:156], float(NE - 1), None, ALU.min))
            own.link(dve.tensor_copy(jobs[0:1, 12:13], end[0:1, 7:8]))
            dve.wait_ge(ht_copied, 4)
            own.link(dve.memset(rt[0:1, 160:161], 0.0))
            dve.memset(rt[0:1, 161:162], 0.0).then_inc(e_lo, RAW_E)
            dve.memset(rt[0:1, 164:165], 0.0).then_inc(e_acc, 4)
            dve.memset(rt[0:1, 162:163], 0.0).then_inc(routed, 1)
            dve.wait_ge(routed, 1)
            n_jobs = dve.value_load(jobs[0:1, 12:13], min_val=1, max_val=MAX_JOBS)

            def one_hot():
                pos, gate = rt[:, 0:4], rt[:, 4:8]
                for n in range(2):
                    own.mark(dve.tensor_scalar(oh[:, n, :], iota, pos[:, n:n + 1], None, ALU.is_equal))
                    own.mark(dve.tensor_scalar(ohg[:, n, :], iota, pos[:, n:n + 1], gate[:, n:n + 1], ALU.is_equal, ALU.mult))
                    own.link(dve.tensor_scalar(oh2[:, n, :], iota, pos[:, 2 + n:3 + n], None, ALU.is_equal))
                own.mark(dve.tensor_tensor(oh, oh, oh2, ALU.add))
                for n in range(2):
                    own.mark(dve.scalar_tensor_tensor(ohg[:, n, :], oh2[:, n, :], gate[:, 2 + n:3 + n], ohg[:, n, :],
                                                      ALU.mult, ALU.add))
                own.link(dve.tensor_scalar(pos, pos, -float(P), None, ALU.add))
                dve.memset(rt[0:1, 163:164], 0.0).then_inc(e_onehot, 1)
                dve.wait_ge(e_onehot, own.jobs_done + 1)

            own.jobs_done = 0
            one_hot()
            own.base, own.k = own.base + own.k, 0
            start = own.base
            dve.wait_ge(yacc_zero, 1)

            def lo(j, i):
                dve.wait_ge(e_hi, j * JOB_SLABS + (i + 1))
                w = wse[i % SPLIT_E]
                dve.tensor_tensor(w[:, 1, :, :], raw_e[i % RAW_E], w[:, 0, :, :], ALU.subtract).then_inc(e_lo, 1)

            def xg_lo(j):
                for n in range(2):
                    dve.wait_ge(e_xghi, 2 * j + (n + 1))
                    dve.tensor_tensor(xg[1][:, 4 * n:4 * n + 4, :], pp[n][:, :].rearrange("p (a b) -> p a b", b=P),
                                      xg[0][:, 4 * n:4 * n + 4, :], ALU.subtract).then_inc(e_xg, 1)

            lo(0, 0)
            xg_lo(0)
            lo(0, 1)
            with dve.Fori(0, n_jobs) as j:
                own.base, own.jobs_done = start + j * (GU_GROUPS + 10), j + 1

                def hT_lo(q):
                    dve.wait_ge(e_hThi, j * GU_GROUPS + (q + 1))
                    dve.tensor_tensor(hT[1][:, 2 * q:2 * q + 2, :], T[q % 2][:, 0:256].rearrange("p (a b) -> p a b", b=P),
                                      hT[0][:, 2 * q:2 * q + 2, :], ALU.subtract).then_inc(e_hT, 1)

                for q in range(GU_GROUPS):
                    lo(j, 2 * q + 2)
                    lo(j, 2 * q + 3)
                    dve.wait_ge(e_tanh, j * GU_GROUPS + (q + 1))
                    own.link(dve.scalar_tensor_tensor(tge[:, q % 2, :], tge[:, q % 2, :], 1.0, S[q % 2][:, 0:256],
                                                      ALU.add, ALU.mult))
                    dve.scalar_tensor_tensor(hse[:, q % 2, :], tge[:, q % 2, :], 0.5, S[q % 2][:, 256:512],
                                             ALU.mult, ALU.mult).then_inc(e_h, 1)
                    if q:
                        hT_lo(q - 1)
                for d in range(DN_SLABS):
                    lo(j, GU_SLABS + d + 2)
                    if d == 0:
                        hT_lo(GU_GROUPS - 1)
                        one_hot()
                xg_lo(j + 1)
                assert own.k == GU_GROUPS + 10
                for n in range(4):
                    dve.wait_ge(e_scat, 4 * j + (n + 1))
                    v = yacc[:, 2 * n:2 * n + 2, :]
                    dve.tensor_tensor(v, [S[0], S[1], T[0], T[1]][n][:, :].rearrange("p (a b) -> p a b", b=SEQ), v,
                                      ALU.add).then_inc(e_acc, 1)
            own.base, own.k = start + n_jobs * (GU_GROUPS + 10), 0
            postnorm(7, 1, 1, SEQ, yacc)

        @block.tensor
        def _(pe):
            mm = pe.matmul

            def split_mm(dst, w_hi, w_lo, x_hi, x_lo, first, last):
                mm(dst, w_hi, x_hi, start=first, stop=False)
                mm(dst, w_hi, x_lo, start=False, stop=False)
                return mm(dst, w_lo, x_hi, start=False, stop=last)

            def first_pair(banks, slots, done):
                for k in range(KT):
                    pe.wait_ge(h_split, 8 * done + k + 1)
                    for bank, slot in zip(banks, slots):
                        ins = split_mm(bank[:, :], wsp[:, slot, 0, P * k:P * k + P], wsp[:, slot, 1, P * k:P * k + P],
                                       hx[:, 0, k, :], hx[:, 1, k, :], k == 0, k == KT - 1)
                        if k == KT - 1:
                            ins.then_inc(tile_done, 1)

            def norm_sum(n, k, N):
                pe.wait_ge(sq_done, 8 * n + k + 1)
                mm(O[1][:, 0:N], mean[:], sq[:, k % 2, 0:N], start=(k == 0), stop=(k == KT - 1)).then_inc(sum_done, 1)

            def ada_product(dst, slots):
                for h in range(2):
                    for k in range(4):
                        for part in range(2):
                            ins = mm(dst[0:4, 0:256], c4[:, 4 * h + k, :], wsp[:, slots[h], part, 256 * k:256 * k + 256],
                                     start=(h + k + part == 0), stop=(h == 1 and k == 3 and part == 1))
                    yield ins

            def ada_turn(dst, col, rows):
                for h in range(2):
                    ins = mm(dst[:, bass.ds(col + 2 * h, 2)], rows[:, P * h:P * h + P], sel[:], start=True, stop=True)
                return ins

            def ada():
                def turn(s):
                    pe.wait_ge(taken[s % 2], s // 2 + 1)
                    ada_turn(T[0], 4 * s, adr_f[:, s % 2, :]).then_inc(cols_done, 1)

                for s in range(ADA_FIRST):
                    if s >= 2:
                        pe.wait_ge(taken[s % 2], s // 2)
                    pe.wait_ge(lo_done, 2 * s + 1)
                    for h, ins in enumerate(ada_product(pp[s % 2], [2 * s % 4, (2 * s + 1) % 4])):
                        ins.then_inc(tile_done, 1)
                        if h == 0:
                            pe.wait_ge(lo_done, 2 * s + 2)
                    for k in FIRST_NORM[s]:
                        norm_sum(0, k, TOK)
                    if s:
                        turn(s - 1)
                turn(ADA_FIRST - 1)

            def attn(l, b, s):
                units = attn_units(l)
                nqt = (TOK if l == 0 else SEQ) // P
                base = unit_base[l, b]
                if s < len(units):
                    tt, half, qt = units[s]
                    w = base + s
                    pe.wait_ge(q2_ready, w + 1)
                    if w >= 2:
                        pe.wait_ge(exp_done, w - 1)
                    if b == 0:
                        wait_taken(pe, step_of[l, "rope_k", 0])
                        keys = ka
                    else:
                        wait_taken(pe, step_of[l, "kn", tt])
                        keys = kn[:, tt, :]
                    k0 = 0 if qt < 2 else SEQ
                    mm(S[w % 2][:, 0:TOK - k0], q2[:, half, w % 2, :], keys[:, k0:TOK], start=True, stop=True
                       ).then_inc(scores_done, 1)
                if 0 <= s - 3 < len(units):
                    w = base + s - 3
                    tt, half, qt = units[s - 3]
                    kts = range(4) if qt < 2 else range(2, 4)
                    ot = otile_base[l, b] + tt
                    pe.wait_ge(pT_copied, w + 1)
                    if half == 0 and qt == 0 and ot >= 2:
                        pe.wait_ge(o_split, ot - 1)
                    if s - 3 == 0:
                        if b == 0:
                            wait_taken(pe, step_of[l, "va_t", 0])
                        else:
                            for key in ((0, 0), (0, 1), (1, 0), (1, 1)):
                                wait_taken(pe, step_of[l, "vn", key])
                    vc = HD * half if b == 0 else P + HD * (2 * tt + half)
                    for n, k in enumerate(kts):
                        ins = mm(O[ot % 2][HD * half:HD * half + HD, P * qt:P * qt + P], V[:, k, vc:vc + HD],
                                 prT[:, w % 2, n, :], start=(n == 0), stop=(n == len(kts) - 1))
                    ins.then_inc(pv_done, 1)
                if 0 <= s - 2 < len(units):
                    w = base + s - 2
                    kts = 4 if units[s - 2][2] < 2 else 2
                    pe.wait_ge(probs_done, w + 1)
                    if w >= 2:
                        pe.wait_ge(pT_copied, w - 1)
                    for k in range(kts):
                        ins = pe.transpose(T[w % 2][:, P * k:P * k + P], pr[:, w % 2, P * k:P * k + P], ident[:])
                    ins.then_inc(pT_done, 1)

            def mixer(l, nn, hs):
                nq = TOK if l == 0 else SEQ
                for row in mixer_steps[l]:
                    for b, s in row["slots"]:
                        attn(l, b, s)
                    what, i, u, bank = row["what"], row["i"], row["u"], row["bank"]
                    dst = pp[bank]
                    if what == "va":
                        continue
                    if what == "ka":
                        if row["use"] > 1:
                            for b in range(2):
                                pe.wait_ge(taken[b], row["use"] - 1)
                        pe.wait_ge(lo_done, u + 2)
                        first_pair([pp[bank], pp[1 - bank]], [u % 4, (u + 1) % 4], hs)
                        continue
                    if row["use"] > 1:
                        pe.wait_ge(taken[bank], row["use"] - 1)
                    if u is not None:
                        pe.wait_ge(lo_done, u + 1 + (what in ("vn", "ada")))
                        slot = u % 4
                    if what == "ada":
                        for ins in ada_product(dst, [u % 4, (u + 1) % 4]):
                            pass
                    elif what == "ada_t":
                        wait_taken(pe, step_of[l, "ada", i])
                        ins = ada_turn(dst, 0, ada_rows(ADA_MIXER.index(i)))
                    elif what in ("rope_q", "rope_k"):
                        wait_taken(pe, step_of[l, "qa" if what == "rope_q" else "ka", i])
                        v = qa[:, i, 0:SEQ] if what == "rope_q" else ka[:, 0:SEQ]
                        if i == 0:
                            pe.wait_ge(consts_in, 16 * 7)
                        ins = mm(dst[:, 0:SEQ], rot[:], v, start=True, stop=True)
                    elif what == "va_t":
                        wait_taken(pe, step_of[l, "va", 0])
                        for k in range(4):
                            ins = pe.transpose(dst[:, P * k:P * k + P], vat[:, P * k:P * k + P], ident[:])
                    elif what == "vn":
                        s, tp = i
                        for q in range(2):
                            tk = slice(P * (2 * tp + q), P * (2 * tp + q) + P)
                            d = dst[:, 256 * q:256 * q + 256]
                            for k in range(KT):
                                sl = (u + k // 4) % 4
                                wh, wl = (wsp[:, sl, part, 256 * (k % 4):256 * (k % 4) + 256] for part in range(2))
                                mm(d, hx[:, 0, k, tk], wh, start=(k == 0), stop=False)
                                mm(d, hx[:, 0, k, tk], wl, start=False, stop=False)
                                ins = mm(d, hx[:, 1, k, tk], wh, start=False, stop=(k == KT - 1))
                    else:
                        if what == "br":
                            x, nk = o_br[i[0]], BT
                            if i[1] == 0:
                                if i[0] == 1:
                                    pe.wait_ge(ob_split, 4 * (l + 1))
                                else:
                                    pe.wait_ge(o_split, otile_base[l, i[0] // 2] + 4)
                        elif what == "wout":
                            x, nk = m_sp, KT
                            if i == 0:
                                pe.wait_ge(m_split, 8 * (l + 1))
                        else:
                            x, nk = hx, KT
                        N = TOK if what in ("ka", "va", "kn") else nq
                        for k in range(nk):
                            ins = split_mm(dst[:, 0:N], wsp[:, slot, 0, P * k:P * k + P], wsp[:, slot, 1, P * k:P * k + P],
                                           x[:, 0, k, 0:N], x[:, 1, k, 0:N], k == 0, k == nk - 1)
                    ins.then_inc(tile_done, 1)
                    if what == "wout" and i:
                        norm_sum(nn, i - 1, nq)
                norm_sum(nn, KT - 1, nq)

            def ffn():
                for h in range(2):
                    u0, nF, f0 = 2 * g_gu[h], F_HALF[h], h * F_HALF[0]

                    def turn(i, s):
                        pe.wait_ge(taken[s], use_gu[h] + i + 1)
                        ada_turn(O[0], 4 * f0 + 8 * i + 4 * s, adr_f[:, s, :]).then_inc(cols_done, 1)

                    def body(i, last, first=False):
                        for s in range(2):
                            if h == 0 and first and s == 0:
                                pe.wait_ge(lo_done, u0 + 2)
                                first_pair([S[0], T[0]], [u0 % 4, (u0 + 1) % 4], 1)
                            for part, bank in ((0, S[s]), (1, T[s])):
                                if h == 0 and first and s == 0:
                                    continue
                                pe.wait_ge(lo_done, u0 + 8 * i + 4 * s + part + 1)
                                if part == 0:
                                    pe.wait_ge(gu_taken, f0 + 2 * i + s + 1)
                                slot = (u0 + 4 * s + part) % 4
                                for k in range(KT):
                                    ins = split_mm(bank[:, :], wsp[:, slot, 0, P * k:P * k + P], wsp[:, slot, 1, P * k:P * k + P],
                                                   hx[:, 0, k, :], hx[:, 1, k, :], k == 0, k == KT - 1)
                                ins.then_inc(tile_done, 1)
                            if s == 1:
                                turn(i, 0)
                            elif not first:
                                turn(i - 1, 1)
                            pe.wait_ge(lo_done, u0 + 8 * i + 4 * s + 4)
                            pe.wait_ge(taken[s], use_gu[h] + i)
                            for ins in ada_product(pp[s], [(u0 + 4 * s + 2) % 4, (u0 + 4 * s + 3) % 4]):
                                ins.then_inc(tile_done, 1)
                    body(0, False, first=True)
                    with pe.Fori(1, nF // 2) as i:
                        body(i, False)
                    turn(nF // 2 - 1, 1)
                    pe.wait_ge(hF_done, f0 + nF)
                    u0 = 2 * g_dn[h]
                    hk = nF // 2

                    def down(i, s):
                        for part in range(2):
                            pe.wait_ge(lo_done, u0 + 4 * i + 2 * s + part + 1)
                            if part == 0:
                                pe.wait_ge(taken[s], use_dn[h] + i)
                            slot = (u0 + 2 * s + part) % 4
                            for k in range(hk):
                                f = part * hk + k
                                ins = split_mm(pp[s][:, :], wsp[:, slot, 0, P * k:P * k + P], wsp[:, slot, 1, P * k:P * k + P],
                                               hF[:, 0, f, :], hF[:, 1, f, :], f == 0, f == nF - 1)
                            ins.then_inc(tile_done, 1)
                    if h == 0:
                        def body(i, last):
                            down(i, 0)
                            down(i, 1)
                        body.own_per = 0
                        loop(pe, DN_STAGE // 2, body)
                    else:
                        for n in range(KT):
                            down(n // 2, n % 2)
                            if n:
                                norm_sum(3, n - 1, TOK)
                norm_sum(3, KT - 1, TOK)

            pe.wait_ge(c_ready, 2)
            pe.wait_ge(eps_ready, 3)
            ada()
            mixer(0, 1, 0)
            for k in range(KT):
                norm_sum(2, k, TOK)
            ffn()
            for k in range(KT):
                norm_sum(4, k, TOK)
            mixer(1, 5, 2)
            for k in range(KT):
                norm_sum(6, k, SEQ)
            pe.wait_ge(affine, 3 * 2 * KT + KT)
            for n in range(4):
                for k in range(4):
                    c = 4 * (n % 2) + k
                    ins = pe.transpose([pp[0], pp[1], S[0], S[1]][n][:, P * k:P * k + P],
                                       hfa[:, c, P * (n // 2):P * (n // 2) + P], ident[:])
                ins.then_inc(rt_pe, 1)
            for n in range(2):
                for k in range(KT):
                    ins = mm(O[0][:, NE * n:NE * n + NE], hfa[:, k, P * n:P * n + P], wr[:, k, :], start=(k == 0), stop=(k == KT - 1))
            ins.then_inc(rt_pe, 1)
            pe.wait_ge(rt_dve, 2)
            A0, A1 = rt[:, 80:88], rt[:, 88:96]
            mm(O[0][:, 32:40], tri, A0, start=True, stop=True)
            mm(O[0][:, 40:48], ones, A0, start=True, stop=False)
            mm(O[0][:, 40:48], tri, A1, start=False, stop=True)
            mm(O[0][:, 48:56], ones, A0, start=True, stop=False)
            mm(O[0][:, 48:56], ones, A1, start=False, stop=True).then_inc(rt_pe, 1)
            pe.wait_ge(routed, 1)
            mm(O[0][:, 56:64], ones, A1, start=True, stop=True).then_inc(e_used, SPLIT_E)
            n_jobs = pe.value_load(jobs[0:1, 12:13], min_val=1, max_val=MAX_JOBS)

            def gather(j):
                pe.wait_ge(e_onehot, j + 1)
                for k in range(KT):
                    for n in range(2):
                        ins = mm(pp[k // 4][:, P * (k % 4):P * (k % 4) + P], ht[:, n, P * k:P * k + P], oh[:, n, :],
                                 start=(n == 0), stop=(n == 1))
                ins.then_inc(e_gath, 1)

            gather(0)
            with pe.Fori(0, n_jobs) as j:
                def got(i):
                    pe.wait_ge(e_lo, j * JOB_SLABS + (i + 1 + RAW_E))

                def transposes(q):
                    pe.wait_ge(e_h, j * GU_GROUPS + (q + 1))
                    if q >= 2:
                        pe.wait_ge(e_hT, j * GU_GROUPS + (q - 1))
                    for n in range(2):
                        ins = pe.transpose(T[q % 2][:, P * n:P * n + P], hse[:, q % 2, P * n:P * n + P], ident[:])
                    ins.then_inc(e_T, 1)

                pe.wait_ge(e_xg, 2 * j + 2)
                for q in range(GU_GROUPS):
                    if q >= 2:
                        pe.wait_ge(e_h, j * GU_GROUPS + (q - 1))
                    else:
                        pe.wait_ge(e_acc, 4 * j + (q + 1))
                    for h in range(2):
                        i = 2 * q + h
                        got(i)
                        w = wse[i % SPLIT_E]
                        for k in range(4):
                            wh, wl = (w[:, part, 2 * k:2 * k + 2, :] for part in range(2))
                            kk = 4 * h + k
                            d = S[q % 2][:, :].rearrange("p (a b) -> p a b", b=256)
                            mm(d, xg[0][:, kk, :], wh, start=(kk == 0), stop=False)
                            mm(d, xg[0][:, kk, :], wl, start=False, stop=False)
                            ins = mm(d, xg[1][:, kk, :], wh, start=False, stop=(kk == KT - 1))
                        ins.then_inc(e_used, 1)
                    if q == 1:
                        pe.wait_ge(e_acc, 4 * j + 4)
                        for n in range(2):
                            ins = pe.transpose(T[1][:, P * n:P * n + P], ohg[:, n, :], ident[:])
                        ins.then_inc(e_gath, 1)
                    if q == 2:
                        pe.wait_ge(e_ohT, j + 1)
                    if q:
                        transposes(q - 1)
                for d_ in range(DN_SLABS):
                    i = GU_SLABS + d_
                    got(i)
                    if d_ == 0:
                        pe.wait_ge(e_hT, j * GU_GROUPS + 1)
                    pe.wait_ge(e_hT, j * GU_GROUPS + (d_ + 1))
                    w = wse[i % SPLIT_E]
                    for f2 in range(2):
                        f = 2 * d_ + f2
                        for x, part in ((0, 0), (0, 1), (1, 0)):
                            for n in range(2):
                                ins = mm(O[n][:, :].rearrange("p (a b) -> p a b", b=256), hT[x][:, f, :],
                                         w[:, part, 4 * f2 + 2 * n:4 * f2 + 2 * n + 2, :],
                                         start=(f == 0 and x == 0 and part == 0), stop=(f == FE_T - 1 and x == 1))
                    ins.then_inc(e_used, 1)
                    if d_ == 0:
                        transposes(GU_GROUPS - 1)
                gather(j + 1)
                for n in range(4):
                    pe.wait_ge(e_yb, 2 * j + (n // 2 + 1))
                    if n == 0:
                        pe.wait_ge(e_hT, (j + 1) * GU_GROUPS)
                    for h in range(2):
                        c = 2 * n + h
                        ins = mm([S[0], S[1], T[0], T[1]][n][:, SEQ * h:SEQ * h + SEQ], yb[:, P * c:P * c + P], ohT,
                                 start=True, stop=True)
                    ins.then_inc(e_scat, 1)
            for k in range(KT):
                norm_sum(7, k, SEQ)


def _tiles(w, cols):
    k = w.shape[0] // P
    return np.stack([w[i * P:(i + 1) * P][:, cols] for i in range(k)], axis=1)


def _pack_dense(inp):
    main, brs = [], []
    qa0, ka0, va0, ux0 = 0, BW, BW + P, BW + 2 * P
    gb0, gc0, qn0, kn0, vn0, gx0 = (ux0 + n * BW for n in range(1, 7))

    def put(*parts):
        main.append(np.concatenate([p.reshape(P, -1) for p in parts], axis=1))

    def ada(l, s):
        put(_tiles(inp["w_ada"][l], slice(256 * s, 256 * s + 256)))

    def mixer(l):
        w = inp["w_in"][l]
        col = lambda c0, i: np.arange(c0 + P * i, c0 + P * i + P)
        two = lambda x, y: put(_tiles(w, x), _tiles(w, y))
        qcol = lambda i: np.concatenate([np.arange(qa0 + HD * i, qa0 + HD * i + HD),
                                         np.arange(qa0 + HD * (i + 4), qa0 + HD * (i + 4) + HD)])
        rest = list(ADA_MIXER if l == 0 else [])

        def beside():
            if rest:
                ada(*rest.pop(0))

        two(col(ka0, 0), col(va0, 0))
        for i in (0, 2):
            two(qcol(i), qcol(i + 1))
        for c in range(BT):
            two(col(ux0, c), col(gc0, c))
            if c >= 2:
                beside()
        for c0 in (gb0, qn0, kn0):
            for i in (0, 2):
                two(col(c0, i), col(c0, i + 1))
                beside()
        for s in range(2):
            put(_tiles(w, slice(vn0 + 256 * s, vn0 + 256 * s + 256)))
        for r in range(3):
            wb = inp["w_branch"][l, r]
            if r == 0:
                wb = wb[np.concatenate([np.arange(HD * h, HD * h + HD) for i in range(4) for h in (i, i + 4)])]
            for n in range(0, KT, 2):
                two(col(gx0 + D * r, n), col(gx0 + D * r, n + 1))
                brs.append(np.concatenate([_tiles(wb, slice(P * m, P * m + P)).reshape(P, -1) for m in (n, n + 1)], axis=1))
                beside()
        wo = inp["w_out"][l]
        for n in range(0, KT, 2):
            put(_tiles(wo, slice(P * n, P * n + P)), _tiles(wo, slice(P * n + P, P * n + 2 * P)))

    for s in range(ADA_FIRST):
        ada(0, s)
    mixer(0)
    gu, dn = inp["w_gu_dense"][0], inp["w_dn_dense"][0]
    dns, f = [], 0
    for nF in F_HALF:
        for j in range(f, f + nF):
            put(_tiles(gu, slice(P * j, P * j + P)), _tiles(gu, slice(FFN_D + P * j, FFN_D + P * j + P)))
            ada(1, ADA_SLABS - ADA_FFN + j)
        dns.append(np.stack([_tiles(dn[P * f:P * (f + nF)], slice(P * n, P * n + P)).reshape(P, -1) for n in range(KT)]))
        f += nF
    mixer(1)
    return np.stack(main), np.stack(brs), dns[0], dns[1]


def _pack_experts(inp):
    out = np.empty((NE, JOB_SLABS, P, 8, 256), np.float32)
    gu, dn = inp["w_gu_moe"][0], inp["w_dn_moe"][0]
    for e in range(NE):
        g = gu[e].reshape(2, 4, P, 2, GU_GROUPS, 256)
        out[e, :GU_SLABS] = g.transpose(4, 0, 2, 1, 3, 5).reshape(GU_SLABS, P, 8, 256)
        d = dn[e].reshape(DN_SLABS, 2, P, D)
        out[e, GU_SLABS:] = d.transpose(0, 2, 1, 3).reshape(DN_SLABS, P, 8, 256)
    return out.reshape(NE * JOB_SLABS, P, 8, 256)


def _shape_constants():
    i = np.arange(P)
    rot = np.zeros((P, P), np.float32)
    for m in range(P):
        q = m % 32
        if q < 16:
            rot[m + 16, m] = -1.0
        else:
            rot[m - 16, m] = 1.0
    half = HD // 2
    inv = 1.0 / (10000.0 ** (np.arange(0, half, 2, dtype=np.float32) / np.float32(half)))
    pos = np.arange(SEQ)
    ar = (pos // GRID_W).astype(np.float32)[:, None] * inv[None].astype(np.float32)
    ac = (pos % GRID_W).astype(np.float32)[:, None] * inv[None].astype(np.float32)
    ang = np.concatenate([ar, ar, ac, ac], axis=-1).astype(np.float32)
    cs = np.stack([np.tile(np.cos(ang).T, (2, 1)), np.tile(np.sin(ang).T, (2, 1))], axis=1).astype(np.float32)
    q, k = i[:, None], i[None, :]
    wmask = np.stack([np.where(k + P - q <= WINDOW, 0.0, -BIG), np.where(q + P - k <= WINDOW, 0.0, -BIG)], axis=1)
    c = np.arange(GRID_W)
    start = np.clip(c - NA_COLS // 2, 0, GRID_W - NA_COLS)
    ok = (c[None, :] >= start[:, None]) & (c[None, :] < start[:, None] + NA_COLS)
    cmask = np.tile(np.where(ok, 0.0, -BIG), (2, 1))
    routing = np.zeros((P, 2, SEQ), np.float32)
    routing[:, 0, 0:P] = i[:, None] < i[None, :]
    routing[:, 0, P:2 * P] = 1.0
    routing[:, 1, 0:P] = i[None, :]
    routing[:, 1, P:P + 8] = np.arange(8)
    routing[:, 1, P + 8:P + 16] = np.arange(8) + 99.0
    routing[:, 1, P + 16:P + 28] = np.arange(12)
    return {"ident": np.eye(P, dtype=np.float32), "rot": rot, "cossin": cs, "wmask": wmask.astype(np.float32),
            "cmask": cmask.astype(np.float32), "routing": routing}


def _position_rows(rpb):
    q, k = np.arange(SEQ)[:, None], np.arange(SEQ)[None, :]
    dr = k // GRID_W - q // GRID_W + RPB_R // 2
    dc = np.clip(k % GRID_W - q % GRID_W, 1 - NA_COLS, NA_COLS - 1) + NA_COLS - 1
    return rpb[:, :, dr, dc].reshape(DEPTH, 8, 2, P, SEQ).transpose(0, 1, 3, 2, 4)


def _lay_out(inp):
    col = lambda v: v.reshape(-1, P).T
    vec = []
    for l in range(DEPTH):
        conv = np.concatenate([col(inp["conv_w"][l, k]) for k in range(3)], axis=1)
        vec.append(np.concatenate([col(inp["g_pre_mix"][l]), col(inp["g_post_mix"][l]), col(inp["g_pre_ffn"][l]),
                                   col(inp["g_post_ffn"][l]), col(inp["b_gate"][l]), col(inp["b_ada"][l]), conv,
                                   np.broadcast_to(inp["sink"][l], (P, 8))], axis=1))
    w_main, w_br, w_dn0, w_dn1 = _pack_dense(inp)
    tok = np.concatenate([inp["x"][0], inp["ctx"][0]], axis=0)
    arrays = {
        "w_main": w_main, "w_br": w_br, "w_dn0": w_dn0, "w_dn1": w_dn1, "w_moe": _pack_experts(inp),
        "x_both": tok.T.reshape(KT, P, TOK).transpose(1, 0, 2),
        "c_both": np.stack([inp["c"][0], inp["c_ctx"]], axis=1).reshape(KT, P, 2).transpose(1, 0, 2),
        "vec": np.stack(vec, axis=1), "rpb_rows": _position_rows(inp["rpb"]),
        "w_router": inp["w_router"][0].reshape(KT, P, NE).transpose(1, 0, 2),
        "b_router": np.broadcast_to(inp["b_router"][0], (P, NE)),
    }
    arrays.update(_shape_constants())
    return {k: np.ascontiguousarray(v) for k, v in arrays.items()}


def kernel(**inputs):
    import concourse.bacc as _bacc
    from concourse import mybir as _mybir
    from concourse.bass_utils import run_bass_kernel_spmd as _run

    arrays = _lay_out({k: np.asarray(v) for k, v in inputs.items()})
    nc = _bacc.Bacc("TRN2", target_bir_lowering=False, num_devices=1)
    aps = {k: nc.dram_tensor(f"in_{k}", v.shape, _mybir.dt.from_np(v.dtype), kind="ExternalInput").ap()
           for k, v in arrays.items()}
    out = nc.dram_tensor("out_x", (P, KT, SEQ), _mybir.dt.float32, kind="ExternalOutput").ap()
    build_program(nc, aps, out)
    r = _run(nc, [{f"in_{k}": v for k, v in arrays.items()}], core_ids=[0])
    got = r.results[0]["out_x"]
    return np.ascontiguousarray(got.transpose(2, 1, 0).reshape(1, SEQ, D))
```
